# Optimizing a Trainium2 kernel written in Bass

```python
import jax, jax.numpy as jnp
from jax import lax
import numpy as np

D_MODEL = 1024
BATCH = 1
SEQ = 512
DEPTH = 1

ATTN_GROUPS = ((128, 1), (512, 4), (2048, 16))
N_ATTN_GROUPS = 3
HEADS_PER_GROUP = 8
HEAD_DIM_A = 64
ATTN_GROUP_WIDTH = HEADS_PER_GROUP * HEAD_DIM_A
ATTN_QKV_WIDTH = N_ATTN_GROUPS * ATTN_GROUP_WIDTH
DN_HEADS = 8
DN_HEAD_DIM = 128
DN_WIDTH = DN_HEADS * DN_HEAD_DIM
CONV_WIDTH = 4
CHUNK = 64
N_EXPERT_GROUPS = 4
EXPERTS_PER_GROUP = 4
N_EXPERTS = N_EXPERT_GROUPS * EXPERTS_PER_GROUP
TOP_K = 2
D_EXPERT = 256
PLE_DIM = 256
EPS = 1e-6
IN_WIDTHS = (3 * ATTN_QKV_WIDTH, 3 * DN_WIDTH, DN_WIDTH, DN_HEADS, DN_HEADS, D_MODEL, D_MODEL)
IN_TOTAL = 3 * ATTN_QKV_WIDTH + 4 * DN_WIDTH + 2 * DN_HEADS + 2 * D_MODEL


def rms_norm(x, gain):
    xf = x.astype(jnp.float32)
    y = xf * lax.rsqrt(jnp.mean(xf * xf, axis=-1, keepdims=True) + EPS)
    return y * gain.astype(jnp.float32)

def l2_norm(x):
    return x * lax.rsqrt(jnp.sum(x * x, axis=-1, keepdims=True) + EPS)

def split_columns(t, widths):
    out, start = [], 0
    for w in widths:
        out.append(t[..., start:start + w])
        start += w
    return out

def dilated_window_attention(q, k, v, window, dilation):
    b, s, h, dh = q.shape
    blk = window // dilation
    span = blk * dilation
    s_pad = -(-s // span) * span
    n_sub = s_pad // dilation
    nblk = n_sub // blk

    def to_blocks(t):
        t = jnp.pad(t, ((0, 0), (0, s_pad - s), (0, 0), (0, 0)))
        t = t.reshape(b, n_sub, dilation, h, dh).transpose(0, 2, 3, 1, 4)
        return t.reshape(b, dilation, h, nblk, blk, dh)

    def with_prev(t):
        prev = jnp.pad(t[:, :, :, :-1], ((0, 0), (0, 0), (0, 0), (1, 0), (0, 0), (0, 0)))
        return jnp.concatenate([prev, t], axis=4)

    qb = to_blocks(q)
    kb = with_prev(to_blocks(k))
    vb = with_prev(to_blocks(v))
    scores = jnp.einsum('brhnqd,brhnkd->brhnqk', qb, kb) * (dh ** -0.5)
    qi = jnp.arange(blk)[:, None]
    kj = jnp.arange(2 * blk)[None, :]
    dist = blk + qi - kj
    band = (dist >= 0) & (dist <= blk)
    has_prev = jnp.arange(nblk)[:, None, None] > 0
    valid = band[None] & (has_prev | (kj >= blk)[None])
    scores = jnp.where(valid, scores, -jnp.inf)
    m = jnp.max(scores, axis=-1, keepdims=True)
    e = jnp.exp(scores - m)
    denom = jnp.sum(e, axis=-1)
    o = jnp.einsum('brhnqk,brhnkd->brhnqd', e, vb) / denom[..., None]
    lse = m[..., 0] + jnp.log(denom)
    o = o.reshape(b, dilation, h, n_sub, dh).transpose(0, 3, 1, 2, 4).reshape(b, s_pad, h, dh)[:, :s]
    lse = lse.reshape(b, dilation, h, n_sub).transpose(0, 3, 1, 2).reshape(b, s_pad, h)[:, :s]
    return o, lse

def causal_short_conv(x, w):
    kw = w.shape[0]
    s = x.shape[1]
    xp = jnp.pad(x, ((0, 0), (kw - 1, 0), (0, 0)))
    y = xp[:, kw - 1:kw - 1 + s] * w[kw - 1]
    for j in range(kw - 1):
        y = y + xp[:, j:j + s] * w[j]
    return jax.nn.silu(y)

def gated_delta_rule(q, k, v, beta, g):
    b, s, h, dk = q.shape
    dv = v.shape[-1]
    n = s // CHUNK

    def chunkify(t):
        return t.reshape(b, n, CHUNK, h, -1).transpose(1, 0, 3, 2, 4)

    qc, kc, vc = chunkify(q), chunkify(k), chunkify(v)
    bc = beta.reshape(b, n, CHUNK, h).transpose(1, 0, 3, 2)
    gcum = jnp.cumsum(g.reshape(b, n, CHUNK, h).transpose(1, 0, 3, 2), axis=-1)
    tril = jnp.tril(jnp.ones((CHUNK, CHUNK), dtype=bool))
    tril_strict = jnp.tril(jnp.ones((CHUNK, CHUNK), dtype=bool), -1)
    decay_mat = jnp.exp(jnp.where(tril, gcum[..., :, None] - gcum[..., None, :], -jnp.inf))
    kbeta = kc * bc[..., None]
    a_mat = jnp.where(tril_strict, jnp.einsum('nbhid,nbhjd->nbhij', kbeta, kc) * decay_mat, 0.0)
    eye = jnp.eye(CHUNK, dtype=jnp.float32)
    t_mat = lax.linalg.triangular_solve(eye + a_mat, jnp.broadcast_to(eye, a_mat.shape),
                                        left_side=True, lower=True, unit_diagonal=True)
    u = jnp.einsum('nbhij,nbhjd->nbhid', t_mat, vc * bc[..., None])
    w = jnp.einsum('nbhij,nbhjd->nbhid', t_mat, kbeta * jnp.exp(gcum)[..., None])
    attn_intra = jnp.where(tril, jnp.einsum('nbhid,nbhjd->nbhij', qc, kc) * decay_mat, 0.0)
    g_last = gcum[..., -1]
    q_dec = qc * jnp.exp(gcum)[..., None]
    k_tail = kc * jnp.exp(g_last[..., None] - gcum)[..., None]

    def step(state, xs):
        qd, ui, wi, ai, gl, kt = xs
        v_new = ui - jnp.einsum('bhcd,bhde->bhce', wi, state)
        o = jnp.einsum('bhcd,bhde->bhce', qd, state) + jnp.einsum('bhij,bhje->bhie', ai, v_new)
        state = state * jnp.exp(gl)[..., None, None] + jnp.einsum('bhcd,bhce->bhde', kt, v_new)
        return state, o

    s0 = jnp.zeros((b, h, dk, dv), jnp.float32)
    _, o = lax.scan(step, s0, (q_dec, u, w, attn_intra, g_last, k_tail))
    return o.transpose(1, 0, 3, 2, 4).reshape(b, s, h, dv)

def hierarchical_moe(hn, w_rg, b_rg, w_re, b_re, w_gate, w_up, w_down):
    bsz, s, d = hn.shape
    t = hn.reshape(-1, d)
    p_group = jax.nn.softmax(t @ w_rg.astype(jnp.float32) + b_rg.astype(jnp.float32), axis=-1)
    g_idx = jnp.argmax(p_group, axis=-1)
    p_g = jnp.take_along_axis(p_group, g_idx[:, None], axis=-1)
    e_logits = (t @ w_re.astype(jnp.float32) + b_re.astype(jnp.float32)).reshape(-1, N_EXPERT_GROUPS, EXPERTS_PER_GROUP)
    sel_logits = jnp.take_along_axis(e_logits, g_idx[:, None, None], axis=1)[:, 0]
    p_exp = jax.nn.softmax(sel_logits, axis=-1)
    top_p, top_i = lax.top_k(p_exp, TOP_K)
    top_p = top_p / jnp.sum(top_p, axis=-1, keepdims=True)
    w_in_group = jnp.sum(jax.nn.one_hot(top_i, EXPERTS_PER_GROUP) * top_p[..., None], axis=1)
    combine = jax.nn.one_hot(g_idx, N_EXPERT_GROUPS)[:, :, None] * (p_g * w_in_group)[:, None, :]
    y = jnp.zeros_like(t)
    for gi in range(N_EXPERT_GROUPS):
        hg = jnp.einsum('td,edf->tef', t, w_gate[gi])
        hu = jnp.einsum('td,edf->tef', t, w_up[gi])
        act = jax.nn.silu(hg) * hu * combine[:, gi, :, None]
        y = y + jnp.einsum('tef,efd->td', act, w_down[gi])
    return y.reshape(bsz, s, d)

def first_inputs(seed: int = 0) -> dict:
    key = jax.random.key(seed)
    ks = jax.random.split(key, 24)
    f32 = jnp.float32

    def nrm(k, shape, scale):
        return jax.random.normal(k, shape, f32) * scale

    def gain(k, n):
        return 1.0 + 0.05 * jax.random.normal(k, (DEPTH, n), f32)

    a_init = jax.random.uniform(ks[6], (DEPTH, DN_HEADS), f32, 1.0, 16.0)
    dt = jnp.exp(jax.random.uniform(ks[7], (DEPTH, DN_HEADS), f32, float(np.log(1e-3)), float(np.log(1e-1))))
    dt_bias = dt + jnp.log(-jnp.expm1(-dt))
    return {
        "x": nrm(ks[0], (BATCH, SEQ, D_MODEL), 1.0),
        "p": nrm(ks[1], (DEPTH, BATCH, SEQ, PLE_DIM), 1.0),
        "norm_mix": gain(ks[2], D_MODEL),
        "w_in": nrm(ks[3], (DEPTH, D_MODEL, IN_TOTAL), D_MODEL ** -0.5),
        "q_norm": gain(ks[4], HEAD_DIM_A),
        "k_norm": gain(ks[5], HEAD_DIM_A),
        "conv_w": nrm(ks[8], (DEPTH, CONV_WIDTH, 3 * DN_WIDTH), CONV_WIDTH ** -0.5),
        "a_log": jnp.log(a_init),
        "dt_bias": dt_bias,
        "dn_out_norm": gain(ks[9], DN_HEAD_DIM),
        "w_branch_a": nrm(ks[10], (DEPTH, ATTN_GROUP_WIDTH, D_MODEL), ATTN_GROUP_WIDTH ** -0.5),
        "w_branch_b": nrm(ks[11], (DEPTH, DN_WIDTH, D_MODEL), DN_WIDTH ** -0.5),
        "w_out": nrm(ks[12], (DEPTH, D_MODEL, D_MODEL), D_MODEL ** -0.5),
        "norm_ffn": gain(ks[13], D_MODEL),
        "w_router_group": nrm(ks[14], (DEPTH, D_MODEL, N_EXPERT_GROUPS), D_MODEL ** -0.5),
        "b_router_group": nrm(ks[15], (DEPTH, N_EXPERT_GROUPS), 0.01),
        "w_router_expert": nrm(ks[16], (DEPTH, D_MODEL, N_EXPERTS), D_MODEL ** -0.5),
        "b_router_expert": nrm(ks[17], (DEPTH, N_EXPERTS), 0.01),
        "w_expert_gate": nrm(ks[18], (DEPTH, N_EXPERT_GROUPS, EXPERTS_PER_GROUP, D_MODEL, D_EXPERT), D_MODEL ** -0.5),
        "w_expert_up": nrm(ks[19], (DEPTH, N_EXPERT_GROUPS, EXPERTS_PER_GROUP, D_MODEL, D_EXPERT), D_MODEL ** -0.5),
        "w_expert_down": nrm(ks[20], (DEPTH, N_EXPERT_GROUPS, EXPERTS_PER_GROUP, D_EXPERT, D_MODEL), D_EXPERT ** -0.5),
        "norm_ple": gain(ks[21], D_MODEL),
        "w_ple": nrm(ks[22], (DEPTH, PLE_DIM, D_MODEL), PLE_DIM ** -0.5),
        "w_ple_gate": nrm(ks[23], (DEPTH, D_MODEL, D_MODEL), D_MODEL ** -0.5),
    }

def first_block(x, p, norm_mix, w_in, q_norm, k_norm, conv_w, a_log, dt_bias, dn_out_norm,
              w_branch_a, w_branch_b, w_out, norm_ffn, w_router_group, b_router_group,
              w_router_expert, b_router_expert, w_expert_gate, w_expert_up, w_expert_down,
              norm_ple, w_ple, w_ple_gate):
    b, s, d = x.shape
    x = x.astype(jnp.float32)
    for i in range(DEPTH):
        h = rms_norm(x, norm_mix[i])
        proj = h @ w_in[i].astype(jnp.float32)
        qkv_a, qkv_b, z_b, beta_b, alpha_b, gate_a, gate_b = split_columns(proj, IN_WIDTHS)

        qkv_a = qkv_a.reshape(b, s, 3, N_ATTN_GROUPS, HEADS_PER_GROUP, HEAD_DIM_A)
        qa = rms_norm(qkv_a[:, :, 0], q_norm[i])
        ka = rms_norm(qkv_a[:, :, 1], k_norm[i])
        va = qkv_a[:, :, 2]
        outs, lses = [], []
        for gi, (win, dil) in enumerate(ATTN_GROUPS):
            o_g, lse_g = dilated_window_attention(qa[:, :, gi], ka[:, :, gi], va[:, :, gi], win, dil)
            outs.append(o_g)
            lses.append(lse_g)
        mix_w = jax.nn.softmax(jnp.stack(lses, axis=0), axis=0)
        o_a = jnp.sum(mix_w[..., None] * jnp.stack(outs, axis=0), axis=0).reshape(b, s, ATTN_GROUP_WIDTH)

        qkv_b = causal_short_conv(qkv_b, conv_w[i].astype(jnp.float32))
        qb, kb, vb = split_columns(qkv_b, (DN_WIDTH, DN_WIDTH, DN_WIDTH))
        qb = l2_norm(qb.reshape(b, s, DN_HEADS, DN_HEAD_DIM)) * (DN_HEAD_DIM ** -0.5)
        kb = l2_norm(kb.reshape(b, s, DN_HEADS, DN_HEAD_DIM))
        vb = vb.reshape(b, s, DN_HEADS, DN_HEAD_DIM)
        beta = jax.nn.sigmoid(beta_b)
        g = -jnp.exp(a_log[i].astype(jnp.float32)) * jax.nn.softplus(alpha_b + dt_bias[i].astype(jnp.float32))
        o_b = gated_delta_rule(qb, kb, vb, beta, g)
        o_b = rms_norm(o_b, dn_out_norm[i]) * jax.nn.silu(z_b.reshape(b, s, DN_HEADS, DN_HEAD_DIM))
        o_b = o_b.reshape(b, s, DN_WIDTH)

        merged = (jax.nn.sigmoid(gate_a) * (o_a @ w_branch_a[i].astype(jnp.float32))
                  + jax.nn.sigmoid(gate_b) * (o_b @ w_branch_b[i].astype(jnp.float32)))
        x = x + merged @ w_out[i].astype(jnp.float32)

        h2 = rms_norm(x, norm_ffn[i])
        x = x + hierarchical_moe(h2, w_router_group[i], b_router_group[i], w_router_expert[i],
                                 b_router_expert[i], w_expert_gate[i].astype(jnp.float32),
                                 w_expert_up[i].astype(jnp.float32), w_expert_down[i].astype(jnp.float32))

        h3 = rms_norm(x, norm_ple[i])
        ple = p[i].astype(jnp.float32) @ w_ple[i].astype(jnp.float32)
        x = x + jax.nn.sigmoid(h3 @ w_ple_gate[i].astype(jnp.float32)) * ple
    return x


DEPTH_2 = 2

LN_EPS = 1e-5
CONV_WIDTH_2 = 512
CONV_K = 31
N_HEADS = 8
QK_NOPE_DIM = 64
QK_ROPE_DIM = 32
V_HEAD_DIM = 64
Q_LORA_RANK = 256
KV_LORA_RANK = 128
ROPE_BASE = 10000.0
Q_BLOCK = 128
ATTN_WIDTH = N_HEADS * V_HEAD_DIM
IN_EVEN = 2 * CONV_WIDTH_2 + Q_LORA_RANK + KV_LORA_RANK + QK_ROPE_DIM
SPLIT_EVEN = [CONV_WIDTH_2, 2 * CONV_WIDTH_2, 2 * CONV_WIDTH_2 + Q_LORA_RANK,
              2 * CONV_WIDTH_2 + Q_LORA_RANK + KV_LORA_RANK]
MIX_EVEN = CONV_WIDTH_2 + ATTN_WIDTH
SSM_WIDTH = 512
SSM_GROUP = 16
SSM_GROUPS = SSM_WIDTH // SSM_GROUP
SSM_STATE = 64
DT_MIN = 0.001
DT_MAX = 0.1
D_FF = 2816
FFN_K = 3


def rms_norm_2(x, g):
    xf = x.astype(jnp.float32)
    y = xf * lax.rsqrt(jnp.mean(xf * xf, axis=-1, keepdims=True) + EPS)
    return (y * g.astype(jnp.float32)).astype(x.dtype)

def layer_norm(x, g, b):
    xf = x.astype(jnp.float32)
    mu = jnp.mean(xf, axis=-1, keepdims=True)
    var = jnp.mean(jnp.square(xf - mu), axis=-1, keepdims=True)
    y = (xf - mu) * lax.rsqrt(var + LN_EPS)
    return (y * g.astype(jnp.float32) + b.astype(jnp.float32)).astype(x.dtype)

def causal_dwconv(u, w, b):
    k, c = w.shape
    y = lax.conv_general_dilated(u, w[:, None, :].astype(u.dtype), window_strides=(1,),
                                 padding=[(k - 1, 0)],
                                 dimension_numbers=('NWC', 'WIO', 'NWC'),
                                 feature_group_count=c)
    return y + b.astype(u.dtype)

def rope(t, pos):
    half = QK_ROPE_DIM // 2
    inv = ROPE_BASE ** (-jnp.arange(half, dtype=jnp.float32) / half)
    ang = pos.astype(jnp.float32)[:, None] * inv[None, :]
    cos, sin = jnp.cos(ang)[:, None, :], jnp.sin(ang)[:, None, :]
    tf = t.astype(jnp.float32)
    t1, t2 = tf[..., :half], tf[..., half:]
    return jnp.concatenate([t1 * cos - t2 * sin, t1 * sin + t2 * cos], axis=-1).astype(t.dtype)

def mla_attention(q_nope, q_rope, k_nope, k_rope, v):
    b, s, h, _ = q_nope.shape
    nb = s // Q_BLOCK
    scale = (QK_NOPE_DIM + QK_ROPE_DIM) ** -0.5
    k_pos = jnp.arange(s)

    def blocks(t):
        return jnp.moveaxis(t.reshape((b, nb, Q_BLOCK) + t.shape[2:]), 1, 0)

    def one_block(args):
        qn, qr, i = args
        scores = (jnp.einsum('bqhd,bkhd->bhqk', qn, k_nope).astype(jnp.float32)
                  + jnp.einsum('bqhr,bkr->bhqk', qr, k_rope).astype(jnp.float32)) * scale
        q_pos = i * Q_BLOCK + jnp.arange(Q_BLOCK)
        mask = k_pos[None, :] <= q_pos[:, None]
        scores = jnp.where(mask[None, None], scores, -jnp.inf)
        p = jax.nn.softmax(scores, axis=-1).astype(v.dtype)
        return jnp.einsum('bhqk,bkhd->bqhd', p, v)

    out = lax.map(one_block, (blocks(q_nope), blocks(q_rope), jnp.arange(nb)))
    return jnp.moveaxis(out, 0, 1).reshape(b, s, h * V_HEAD_DIM)

def conv_attn_mixer(xn, w_in, conv_w, conv_b, conv_ln_g, conv_ln_b,
                    q_norm, kv_norm, w_uq, w_ukv, w_out):
    b, s, _ = xn.shape
    h = xn @ w_in
    glu_a, glu_g, c_q, c_kv, k_r = jnp.split(h, SPLIT_EVEN, axis=-1)
    u = glu_a * jax.nn.sigmoid(glu_g)
    u = causal_dwconv(u, conv_w, conv_b)
    u = jax.nn.silu(layer_norm(u, conv_ln_g, conv_ln_b))
    pos = jnp.arange(s)
    q = (rms_norm_2(c_q, q_norm) @ w_uq).reshape(b, s, N_HEADS, QK_NOPE_DIM + QK_ROPE_DIM)
    q_nope, q_rope = q[..., :QK_NOPE_DIM], rope(q[..., QK_NOPE_DIM:], pos)
    kv = (rms_norm_2(c_kv, kv_norm) @ w_ukv).reshape(b, s, N_HEADS, QK_NOPE_DIM + V_HEAD_DIM)
    k_nope, v = kv[..., :QK_NOPE_DIM], kv[..., QK_NOPE_DIM:]
    k_rope = rope(k_r[:, :, None, :], pos)[:, :, 0, :]
    attn = mla_attention(q_nope, q_rope, k_nope, k_rope, v)
    return jnp.concatenate([u, attn], axis=-1) @ w_out

def s5_mixer(xn, w_in, log_dt, a_re, a_im, b_re, b_im, c_re, c_im, d_skip, w_glu, b_glu):
    f32 = jnp.float32
    bsz, s, _ = xn.shape
    u = (xn @ w_in).astype(f32).reshape(bsz, s, SSM_GROUPS, SSM_GROUP)
    dt = jnp.exp(log_dt.astype(f32))[:, None]
    ar, ai = a_re.astype(f32), a_im.astype(f32)
    mag = jnp.exp(ar * dt)
    lb_re, lb_im = mag * jnp.cos(ai * dt), mag * jnp.sin(ai * dt)
    den = ar * ar + ai * ai
    nr, ni = lb_re - 1.0, lb_im
    f_re = (nr * ar + ni * ai) / den
    f_im = (ni * ar - nr * ai) / den
    br, bi = b_re.astype(f32), b_im.astype(f32)
    bb_re = f_re[..., None] * br - f_im[..., None] * bi
    bb_im = f_re[..., None] * bi + f_im[..., None] * br
    bu_re = jnp.einsum('bsgc,gpc->bsgp', u, bb_re)
    bu_im = jnp.einsum('bsgc,gpc->bsgp', u, bb_im)
    lam_re = jnp.broadcast_to(lb_re, bu_re.shape)
    lam_im = jnp.broadcast_to(lb_im, bu_re.shape)

    def combine(e1, e2):
        a1r, a1i, b1r, b1i = e1
        a2r, a2i, b2r, b2i = e2
        return (a2r * a1r - a2i * a1i, a2r * a1i + a2i * a1r,
                a2r * b1r - a2i * b1i + b2r, a2r * b1i + a2i * b1r + b2i)

    _, _, x_re, x_im = lax.associative_scan(combine, (lam_re, lam_im, bu_re, bu_im), axis=1)
    y = (jnp.einsum('gcp,bsgp->bsgc', c_re.astype(f32), x_re)
         - jnp.einsum('gcp,bsgp->bsgc', c_im.astype(f32), x_im)
         + d_skip.astype(f32).reshape(SSM_GROUPS, SSM_GROUP) * u)
    y = jax.nn.gelu(y.reshape(bsz, s, SSM_WIDTH)).astype(xn.dtype)
    z = y @ w_glu + b_glu
    return z[..., :D_MODEL] * jax.nn.sigmoid(z[..., D_MODEL:])

def conv_ffn(xn, w_up, conv_w, conv_b, w_down):
    h = causal_dwconv(xn @ w_up, conv_w, conv_b)
    return (jax.nn.silu(h[..., :D_FF]) * h[..., D_FF:]) @ w_down

def second_inputs(seed: int = 0) -> dict:
    key = jax.random.key(seed)
    keys = iter(jax.random.split(key, 64))
    f32 = jnp.float32

    def nrm(shape, scale):
        return jax.random.normal(next(keys), shape, f32) * scale

    def gain(n):
        return 1.0 + nrm((n,), 0.01)

    d = D_MODEL
    inp = {}
    inp["x"] = nrm((BATCH, SEQ, d), 1.0)
    inp["l0_mix_norm"] = gain(d)
    inp["l0_w_in"] = nrm((d, IN_EVEN), d ** -0.5)
    inp["l0_conv_w"] = nrm((CONV_K, CONV_WIDTH_2), CONV_K ** -0.5)
    inp["l0_conv_b"] = nrm((CONV_WIDTH_2,), 0.01)
    inp["l0_conv_ln_g"] = gain(CONV_WIDTH_2)
    inp["l0_conv_ln_b"] = nrm((CONV_WIDTH_2,), 0.01)
    inp["l0_q_norm"] = gain(Q_LORA_RANK)
    inp["l0_kv_norm"] = gain(KV_LORA_RANK)
    inp["l0_w_uq"] = nrm((Q_LORA_RANK, N_HEADS * (QK_NOPE_DIM + QK_ROPE_DIM)), Q_LORA_RANK ** -0.5)
    inp["l0_w_ukv"] = nrm((KV_LORA_RANK, N_HEADS * (QK_NOPE_DIM + V_HEAD_DIM)), KV_LORA_RANK ** -0.5)
    inp["l0_w_out"] = nrm((MIX_EVEN, d), MIX_EVEN ** -0.5)
    inp["l0_ffn_norm"] = gain(d)
    inp["l0_w_up"] = nrm((d, 2 * D_FF), d ** -0.5)
    inp["l0_ffn_conv_w"] = nrm((FFN_K, 2 * D_FF), FFN_K ** -0.5)
    inp["l0_ffn_conv_b"] = nrm((2 * D_FF,), 0.01)
    inp["l0_w_down"] = nrm((D_FF, d), D_FF ** -0.5)
    inp["l1_mix_norm"] = gain(d)
    inp["l1_w_in"] = nrm((d, SSM_WIDTH), d ** -0.5)
    inp["l1_log_dt"] = jax.random.uniform(next(keys), (SSM_GROUPS,), f32,
                                          float(np.log(DT_MIN)), float(np.log(DT_MAX)))
    inp["l1_a_re"] = -0.5 + nrm((SSM_GROUPS, SSM_STATE), 0.01)
    inp["l1_a_im"] = (jnp.pi * jnp.arange(SSM_STATE, dtype=f32))[None, :] + nrm((SSM_GROUPS, SSM_STATE), 0.01)
    inp["l1_b_re"] = nrm((SSM_GROUPS, SSM_STATE, SSM_GROUP), (2 * SSM_GROUP) ** -0.5)
    inp["l1_b_im"] = nrm((SSM_GROUPS, SSM_STATE, SSM_GROUP), (2 * SSM_GROUP) ** -0.5)
    inp["l1_c_re"] = nrm((SSM_GROUPS, SSM_GROUP, SSM_STATE), SSM_STATE ** -0.5)
    inp["l1_c_im"] = nrm((SSM_GROUPS, SSM_GROUP, SSM_STATE), SSM_STATE ** -0.5)
    inp["l1_d"] = nrm((SSM_WIDTH,), 1.0)
    inp["l1_w_glu"] = nrm((SSM_WIDTH, 2 * d), SSM_WIDTH ** -0.5)
    inp["l1_b_glu"] = nrm((2 * d,), 0.01)
    inp["l1_ffn_norm"] = gain(d)
    inp["l1_w_up"] = nrm((d, 2 * D_FF), d ** -0.5)
    inp["l1_ffn_conv_w"] = nrm((FFN_K, 2 * D_FF), FFN_K ** -0.5)
    inp["l1_ffn_conv_b"] = nrm((2 * D_FF,), 0.01)
    inp["l1_w_down"] = nrm((D_FF, d), D_FF ** -0.5)
    inp["final_norm"] = gain(d)
    return inp

def second_block(x,
              l0_mix_norm, l0_w_in, l0_conv_w, l0_conv_b, l0_conv_ln_g, l0_conv_ln_b,
              l0_q_norm, l0_kv_norm, l0_w_uq, l0_w_ukv, l0_w_out,
              l0_ffn_norm, l0_w_up, l0_ffn_conv_w, l0_ffn_conv_b, l0_w_down,
              l1_mix_norm, l1_w_in, l1_log_dt, l1_a_re, l1_a_im, l1_b_re, l1_b_im,
              l1_c_re, l1_c_im, l1_d, l1_w_glu, l1_b_glu,
              l1_ffn_norm, l1_w_up, l1_ffn_conv_w, l1_ffn_conv_b, l1_w_down,
              final_norm):
    layers = [
        (conv_attn_mixer,
         (l0_w_in, l0_conv_w, l0_conv_b, l0_conv_ln_g, l0_conv_ln_b,
          l0_q_norm, l0_kv_norm, l0_w_uq, l0_w_ukv, l0_w_out),
         l0_mix_norm, (l0_w_up, l0_ffn_conv_w, l0_ffn_conv_b, l0_w_down), l0_ffn_norm),
        (s5_mixer,
         (l1_w_in, l1_log_dt, l1_a_re, l1_a_im, l1_b_re, l1_b_im,
          l1_c_re, l1_c_im, l1_d, l1_w_glu, l1_b_glu),
         l1_mix_norm, (l1_w_up, l1_ffn_conv_w, l1_ffn_conv_b, l1_w_down), l1_ffn_norm),
    ]
    for i in range(DEPTH_2):
        mixer, mix_params, mix_g, ffn_params, ffn_g = layers[i]
        x = x + mixer(rms_norm_2(x, mix_g), *mix_params)
        x = x + conv_ffn(rms_norm_2(x, ffn_g), *ffn_params)
    return rms_norm_2(x, final_norm)


_first_inputs = second_inputs


def second_inputs(seed=0):
    import zlib

    import numpy as np

    out = dict(_first_inputs(seed))
    spreads = {}
    factors = {'l0_mix_norm': 8.0,
     'l0_conv_b': 6.073,
     'l0_conv_ln_g': 8.0,
     'l0_conv_ln_b': 8.0,
     'l0_q_norm': 8.0,
     'l0_kv_norm': 8.0,
     'l0_ffn_norm': 7.552,
     'l0_ffn_conv_b': 7.418,
     'l1_mix_norm': 8.0,
     'l1_a_re': 8.0,
     'l1_b_re': 2.909,
     'l1_b_im': 3.004,
     'l1_c_re': 2.896,
     'l1_c_im': 2.969,
     'l1_b_glu': 8.0,
     'l1_ffn_norm': 8.0,
     'l1_ffn_conv_b': 8.0,
     'final_norm': 5.694}
    for name, (base, spread) in spreads.items():
        noise = np.random.default_rng([zlib.crc32(name.encode()), seed]).standard_normal(out[name].shape)
        drawn = base * np.exp(spread * noise) if base else spread * noise
        out[name] = __import__('jax').numpy.asarray(drawn.astype(out[name].dtype))
    for name, factor in factors.items():
        out[name] = (out[name] * factor).astype(out[name].dtype)
    return out


_narrow_inputs = second_inputs


def second_inputs(seed=0):
    out = dict(_narrow_inputs(seed))
    wider = {'l0_conv_b': 5.04,
     'l0_conv_ln_g': 6.15,
     'l0_conv_ln_b': 5.86,
     'l0_ffn_norm': 3.74,
     'l0_ffn_conv_b': 3.56,
     'l1_mix_norm': 12.0,
     'l1_a_re': 12.0,
     'l1_b_glu': 12.0,
     'l1_ffn_norm': 6.24,
     'l1_ffn_conv_b': 6.07,
     'final_norm': 6.41}
    for name, times in wider.items():
        mean = out[name].mean()
        out[name] = (mean + times * (out[name] - mean)).astype(out[name].dtype)
    return out


def setup_inputs(seed=0):
    out = dict(first_inputs(seed))
    for name, value in second_inputs(seed + 1).items():
        if name != "x":
            out[name + "_2"] = value
    return out


def reference(
    x, p, norm_mix, w_in, q_norm, k_norm, conv_w, a_log, dt_bias, dn_out_norm, w_branch_a,
    w_branch_b, w_out, norm_ffn, w_router_group, b_router_group, w_router_expert,
    b_router_expert, w_expert_gate, w_expert_up, w_expert_down, norm_ple, w_ple, w_ple_gate,
    l0_mix_norm_2, l0_w_in_2, l0_conv_w_2, l0_conv_b_2, l0_conv_ln_g_2, l0_conv_ln_b_2,
    l0_q_norm_2, l0_kv_norm_2, l0_w_uq_2, l0_w_ukv_2, l0_w_out_2, l0_ffn_norm_2, l0_w_up_2,
    l0_ffn_conv_w_2, l0_ffn_conv_b_2, l0_w_down_2, l1_mix_norm_2, l1_w_in_2, l1_log_dt_2,
    l1_a_re_2, l1_a_im_2, l1_b_re_2, l1_b_im_2, l1_c_re_2, l1_c_im_2, l1_d_2, l1_w_glu_2,
    l1_b_glu_2, l1_ffn_norm_2, l1_w_up_2, l1_ffn_conv_w_2, l1_ffn_conv_b_2, l1_w_down_2,
    final_norm_2,
):
    x = first_block(
        x, p, norm_mix, w_in, q_norm, k_norm, conv_w, a_log, dt_bias, dn_out_norm, w_branch_a,
        w_branch_b, w_out, norm_ffn, w_router_group, b_router_group, w_router_expert,
        b_router_expert, w_expert_gate, w_expert_up, w_expert_down, norm_ple, w_ple, w_ple_gate,
    )
    return second_block(
        x, l0_mix_norm_2, l0_w_in_2, l0_conv_w_2, l0_conv_b_2, l0_conv_ln_g_2, l0_conv_ln_b_2,
        l0_q_norm_2, l0_kv_norm_2, l0_w_uq_2, l0_w_ukv_2, l0_w_out_2, l0_ffn_norm_2, l0_w_up_2,
        l0_ffn_conv_w_2, l0_ffn_conv_b_2, l0_w_down_2, l1_mix_norm_2, l1_w_in_2, l1_log_dt_2,
        l1_a_re_2, l1_a_im_2, l1_b_re_2, l1_b_im_2, l1_c_re_2, l1_c_im_2, l1_d_2, l1_w_glu_2,
        l1_b_glu_2, l1_ffn_norm_2, l1_w_up_2, l1_ffn_conv_w_2, l1_ffn_conv_b_2, l1_w_down_2,
        final_norm_2,
    )


_drawn_inputs = setup_inputs


def setup_inputs(seed=0):
    import zlib

    import numpy as np

    out = dict(_drawn_inputs(seed))
    spreads = {}
    factors = {'b_router_group': 8.0, 'l1_mix_norm_2': 2.808, 'l1_a_re_2': 6.339}
    for name, (base, spread) in spreads.items():
        noise = np.random.default_rng([zlib.crc32(name.encode()), seed]).standard_normal(out[name].shape)
        drawn = base * np.exp(spread * noise) if base else spread * noise
        out[name] = __import__('jax').numpy.asarray(drawn.astype(out[name].dtype))
    for name, factor in factors.items():
        out[name] = (out[name] * factor).astype(out[name].dtype)
    return out
```

```python
from contextlib import ExitStack, contextmanager

import numpy as np

import concourse.bass as bass
from concourse import mybir

F32 = mybir.dt.float32
I32 = mybir.dt.int32
ALU = mybir.AluOpType
ACT = mybir.ActivationFunctionType
AX_X = mybir.AxisListType.X

P = 128
T = 512
NB = T // P
D = 1024
DC = D // P
RING = 4
BLOCKS = 16
SLOT = BLOCKS * P
EPS = 1e-6
LN_EPS = 1e-5
NEG = -1e30
GROUPS = 3
AH, AD = 8, 64
DH, DD, CH = 8, 128, 64
FF = 2816
FC = FF // P
MH, NOPE, ROPE, VD = 8, 64, 32, 64


class Count:

    def __init__(self, n=0):
        self.n, self.i, self.per = n, None, 0

    def at(self, k=0):
        v = self.n + k
        return v if self.i is None else self.i * self.per + v

    def next(self):
        self.n += 1
        return self.at()


class Counts(dict):

    def __missing__(self, name):
        self[name] = Count()
        return self[name]


@contextmanager
def loop(e, times, **per):
    counts = e.c
    for k in per:
        counts[k]
    start = {k: c.n for k, c in counts.items()}
    with e.eng.Fori(0, times) as i:
        for k, n in per.items():
            counts[k].i, counts[k].per = i, n
        e.in_loop = i
        yield i
        e.in_loop = None
        grown = {k: c.n - start.get(k, 0) for k, c in counts.items() if c.n != start.get(k, 0)}
        assert grown == per, (e.name, grown, per)
        for k in per:
            counts[k].i = None
    for k, n in per.items():
        counts[k].n += n * (times - 1)


def vector_columns():
    at, n = {}, 0
    for name, w in [("norm_mix", DC), ("q_norm", 1), ("k_norm", 1), ("conv_w", 24 * 4), ("a_log", 1),
                    ("dt_bias", 1), ("dn_out_norm", 1), ("norm_ffn", DC), ("norm_ple", DC),
                    ("mix0", DC), ("conv0_w", 4 * 31), ("conv0_b", 4), ("ln_g", 4), ("ln_b", 4),
                    ("mla_q", 2), ("mla_kv", 1), ("ffn0", DC), ("f0_w", 2 * FC * 3), ("f0_b", 2 * FC),
                    ("mix1", DC), ("s_d", 4), ("glu_b", 16), ("ffn1", DC), ("f1_w", 2 * FC * 3),
                    ("f1_b", 2 * FC), ("final", DC), ("s_dt", 16), ("s_are", 16), ("s_aim", 16),
                    ("b_router", 20)]:
        at[name] = (n, n + w)
        n += w
    return at, n


VEC, NVEC = vector_columns()


def const_columns():
    at, n = {}, 0
    for name, w in [("ident", P), ("ones", P), ("pair_ones", P), ("attn_mask", 4 * 768), ("mla_mask", P),
                    ("rope_cos", T), ("rope_sin", T), ("rope_rot", 96), ("level", 6 * P),
                    ("decay_mask", P), ("strict", P), ("not_start", T), ("first4", 4)]:
        at[name] = (n, n + w)
        n += w
    return at, n


CON, NCON = const_columns()


def constants():
    c = np.zeros((P, NCON), np.float32)

    def put(name, a):
        lo, hi = CON[name]
        a = np.asarray(a, np.float32)
        c[:a.shape[0], lo:hi] = a.reshape(a.shape[0], -1)

    i = np.arange(P)
    put("ident", np.eye(P))
    put("ones", np.ones((P, P)))
    put("pair_ones", (i[:, None] // 64 == i[None] // 64))
    m = np.zeros((P, 4, 768))
    for r in range(4):
        q = 4 * i + r
        d = q[:, None] - np.arange(T)[None]
        m[:, r, 0:512] = np.where((d >= 0) & (d <= 128), 0, NEG)
        m[:, r, 512:640] = np.where(i[:, None] >= i[None], 0, NEG)
        m[:, r, 640:768] = np.where((i[:, None] >= i[None]) & ((i[:, None] - i[None]) % 4 == 0), 0, NEG)
    put("attn_mask", m)
    put("mla_mask", np.where(i[:, None] >= i[None], 0, NEG))
    half = ROPE // 2
    inv = (10000.0 ** (-np.arange(half, dtype=np.float32) / half)).astype(np.float32)
    ang = (np.arange(T, dtype=np.float32)[:, None] * inv[None]).astype(np.float32)
    cos, sin = np.cos(ang).T, np.sin(ang).T
    put("rope_cos", np.concatenate([np.ones((64, T)), cos, cos]))
    put("rope_sin", np.concatenate([np.zeros((64, T)), sin, sin]))
    rot = np.zeros((96, 96))
    for j in range(half):
        rot[64 + half + j, 64 + j] = -1.0
        rot[64 + j, 64 + half + j] = 1.0
    put("rope_rot", rot)
    lv = np.zeros((P, 6, P))
    for n in range(6):
        b = 1 << n
        lv[:, n] = (i[:, None] // (2 * b) == i[None] // (2 * b)) & ((i[:, None] // b) % 2 == 0) & ((i[None] // b) % 2 == 1)
    put("level", lv)
    same = i[:, None] // CH == i[None] // CH
    put("decay_mask", np.where(same & (i[None] >= i[:, None]), 0, NEG))
    put("strict", same & (i[None] > i[:, None]))
    put("not_start", np.broadcast_to(np.arange(T) % CH != 0, (P, T)))
    put("first4", np.broadcast_to([4.0, 3.0, 2.0, 1.0], (P, 4)))
    return c


def weight_stream(w):
    fills = []

    def fill(*parts):
        f = np.zeros((P, SLOT), np.float32)
        at = 0
        for a in parts:
            for k in range(0, a.shape[0], P):
                rows = a[k:k + P]
                f[:rows.shape[0], at:at + rows.shape[1]] = rows
                at += -(-rows.shape[1] // P) * P
        assert at <= SLOT
        fills.append(f)

    w_in = w["w_in"][0]
    qkv = w_in[:, :4608].reshape(D, 3, GROUPS, AH * AD)
    for g in range(GROUPS):
        for half in range(2):
            fill(qkv[512 * half:512 * half + 512, 2, g])
    for pair in range(4):
        cols = slice(128 * pair, 128 * pair + 128)
        for g in range(GROUPS):
            fill(qkv[:, 0, g, cols], qkv[:, 1, g, cols])
        fill()
    o = 4608
    b_qkv = w_in[:, o:o + 3072]
    z = w_in[:, o + 3072:o + 4096]
    o += 4096
    fill(w_in[:, o:o + 8], w_in[:, o + 8:o + 16])
    for h in range(DH):
        c = slice(128 * h, 128 * h + 128)
        fill(b_qkv[:, 0:1024][:, c], b_qkv[:, 1024:2048][:, c])
        fill(b_qkv[:, 2048:3072][:, c], z[:, c])
    ga, gb = w_in[:, o + 16:o + 16 + D], w_in[:, o + 16 + D:o + 16 + 2 * D]
    for m in range(DC):
        c = slice(P * m, P * m + P)
        fill(ga[:, c], gb[:, c])
        fill(w["w_branch_a"][0][:, c], w["w_branch_b"][0][:, c])
    for m in range(0, DC, 2):
        fill(w["w_out"][0][:, P * m:P * m + P], w["w_out"][0][:, P * m + P:P * m + 2 * P])
    fill(np.concatenate([w["w_router_group"][0], w["w_router_expert"][0]], axis=1))
    for g in range(4):
        for e in range(4):
            for j in range(2):
                c = slice(P * j, P * j + P)
                fill(w["w_expert_gate"][0, g, e][:, c], w["w_expert_up"][0, g, e][:, c])
        dn = w["w_expert_down"][0, g].reshape(1024, D)
        for m in range(0, DC, 2):
            fill(dn[:, P * m:P * m + P], dn[:, P * m + P:P * m + 2 * P])
    for m in range(DC):
        c = slice(P * m, P * m + P)
        fill(w["w_ple_gate"][0][:, c], w["w_ple"][0][:, c])

    def ffn(up, down):
        for j in range(FC):
            fill(up[:, P * j:P * j + P], up[:, FF + P * j:FF + P * j + P])
        for m in range(DC):
            c = slice(P * m, P * m + P)
            fill(down[:FF // 2, c])
            fill(down[FF // 2:, c])

    w0 = w["l0_w_in_2"]
    for j in range(4):
        fill(w0[:, P * j:P * j + P], w0[:, 512 + P * j:512 + P * j + P])
    fill(w0[:, 1024:1152], w0[:, 1152:1280])
    fill(w0[:, 1280:1408], np.concatenate([np.zeros((D, 64), np.float32), w0[:, 1408:1440]], axis=1))
    uq = w["l0_w_uq_2"]
    fill(*[uq[:, 96 * h:96 * h + 96] for h in range(MH)])
    ukv = w["l0_w_ukv_2"].reshape(128, MH, 2, 64)
    fill(*[ukv[:, h, 0] for h in range(MH)], np.ascontiguousarray(ukv[:, :, 1]).reshape(128, 512))
    wo = w["l0_w_out_2"]
    for m in range(0, DC, 2):
        fill(wo[:, P * m:P * m + P], wo[:, P * m + P:P * m + 2 * P])
    ffn(w["l0_w_up_2"], w["l0_w_down_2"])
    w1 = w["l1_w_in_2"]
    for m in range(0, 4, 2):
        fill(w1[:, P * m:P * m + P], w1[:, P * m + P:P * m + 2 * P])
    gl = w["l1_w_glu_2"]
    for m in range(0, DC, 2):
        fill(*[gl[:, o + P * j:o + P * j + P] for j in (m, m + 1) for o in (0, D)])
    ffn(w["l1_w_up_2"], w["l1_w_down_2"])
    while len(fills) % RING:
        fill()
    return np.stack(fills)


def vectors(w):
    v = np.zeros((P, NVEC), np.float32)

    def put(name, a):
        lo, hi = VEC[name]
        v[:a.shape[0], lo:hi] = a.reshape(a.shape[0], -1)

    def chunks(a):
        return a.reshape(-1, P).T

    put("norm_mix", chunks(w["norm_mix"][0]))
    put("q_norm", np.tile(w["q_norm"][0], 2)[:, None])
    put("k_norm", np.tile(w["k_norm"][0], 2)[:, None])
    put("conv_w", w["conv_w"][0].reshape(4, 24, P).transpose(2, 1, 0))
    put("a_log", w["a_log"][0][:, None])
    put("dt_bias", w["dt_bias"][0][:, None])
    put("dn_out_norm", w["dn_out_norm"][0][:, None])
    put("norm_ffn", chunks(w["norm_ffn"][0]))
    put("norm_ple", chunks(w["norm_ple"][0]))
    put("mix0", chunks(w["l0_mix_norm_2"]))
    put("conv0_w", w["l0_conv_w_2"].reshape(31, 4, P).transpose(2, 1, 0))
    put("conv0_b", chunks(w["l0_conv_b_2"]))
    put("ln_g", chunks(w["l0_conv_ln_g_2"]))
    put("ln_b", chunks(w["l0_conv_ln_b_2"]))
    put("mla_q", chunks(w["l0_q_norm_2"]))
    put("mla_kv", chunks(w["l0_kv_norm_2"]))
    for n in (0, 1):
        put(f"ffn{n}", chunks(w[f"l{n}_ffn_norm_2"]))
        put(f"f{n}_w", w[f"l{n}_ffn_conv_w_2"].reshape(3, 2, FC, P).transpose(3, 2, 1, 0))
        put(f"f{n}_b", w[f"l{n}_ffn_conv_b_2"].reshape(2, FC, P).transpose(2, 1, 0))
    put("mix1", chunks(w["l1_mix_norm_2"]))
    put("s_d", chunks(w["l1_d_2"]))
    put("glu_b", chunks(w["l1_b_glu_2"]))
    put("final", chunks(w["final_norm_2"]))

    def states(a):
        return a.reshape(16, P).T

    put("s_dt", np.repeat(w["l1_log_dt_2"].reshape(16, 2), 64, axis=1).T)
    put("s_are", states(w["l1_a_re_2"]))
    put("s_aim", states(w["l1_a_im_2"]))
    put("b_router", np.tile(np.concatenate([w["b_router_group"][0], w["b_router_expert"][0]])[None], (P, 1)))
    return v


def ssm_matrices(w):
    out = np.zeros((P, 4, 16, 16), np.float32)
    for n, name in enumerate(("l1_b_re_2", "l1_b_im_2")):
        out[:, n] = w[name].reshape(16, P, 16).transpose(1, 0, 2)
    for n, name in enumerate(("l1_c_re_2", "l1_c_im_2")):
        out[:, 2 + n] = w[name].transpose(0, 2, 1).reshape(16, P, 16).transpose(1, 0, 2)
    return out


class Engine:

    def __init__(self, name, eng, S, acc):
        self.name, self.eng, self.S, self.acc = name, eng, S, acc
        self.c = Counts()
        self.in_loop = None
        self.slot_starts = False
        self.marks = []

    def result(self):
        return self.acc[:, (self.c["tile"].n - 1) % 2, :]

    def skip(self, n=1):
        self.c["tile"].n += n

    def mark(self, name):
        self.marks.append((name, self.c["tile"].n))


class Vector(Engine):
    n_ticks = 0

    @property
    def ticks(self):
        self.n_ticks += 1
        n = self.n_ticks % self.tick_columns.shape[1]
        return self.tick_columns[:, n:n + 1]

    def tick(self):
        self.eng.memset(self.ticks, 0.0).then_inc(self.S["stage"], 1)


class Tensor(Engine):
    def bank(self):
        self.c["tile"].n += 1
        return self.result()

    def landing(self):
        return "loaded%d" % (self.c["fill"].n % RING)

    def landed(self):
        f = self.c["fill"]
        value = 16 * (f.n // RING + 1)
        return value if f.i is None else f.i * (16 * f.per // RING) + value

    def slot(self, ring):
        self.c["fill"].n += 1
        self.slot_starts = True
        return ring[:, (self.c["fill"].n - 1) % RING, :]

    def mm(self, out, lhsT, rhs, start=True, stop=True):
        ins = self.eng.matmul(out, lhsT, rhs, start=start, stop=stop)
        if self.slot_starts:
            self.slot_starts = False
            return ins.then_inc(self.S["slot_free"], 1)
        return ins

    def dense(self, out, weights, moving):
        for k in range(len(weights)):
            ins = self.mm(out, weights[k], moving[k], k == 0, k == len(weights) - 1)
        ins.then_inc(self.S["tile_done"], 1)


def blocks(slot, first, n, width=P):
    return [slot[:, P * (first + k):P * (first + k) + width] for k in range(n)]


def program(nc, x, p, stream, vecs, consts, ssm, out):
    with ExitStack() as ctx:
        def sb(name, shape, dt=F32):
            return ctx.enter_context(nc.sbuf_tensor(name, shape, dt))

        class Sems(dict):
            def __missing__(self, name):
                self[name] = ctx.enter_context(nc.semaphore("s_" + name))
                return self[name]

        S = Sems()
        NF = stream.shape[0]
        ring = sb("ring", [P, RING, SLOT])
        xT = sb("xT", [P, DC, T])
        hT = sb("hT", [P, DC, T])
        mixT = sb("mixT", [P, 12, T])
        con = sb("con", [P, NCON])
        vec = sb("vec", [P, NVEC])
        WORK = 23500
        work = sb("work", [P, WORK])
        acc = ctx.enter_context(nc.psum_tensor("acc", [P, 2, 512], F32))
        bank = ctx.enter_context(nc.psum_tensor("bank", [P, 6, 512], F32))
        flat = bank[:, :, :].rearrange("p b n -> p (b n)")

        def C(name, rows=P):
            lo, hi = CON[name]
            return con[0:rows, lo:hi]

        def V(name):
            lo, hi = VEC[name]
            return vec[:, lo:hi]

        ident, ones, pair_ones = C("ident"), C("ones"), C("pair_ones")

        class Arena:

            def __init__(self, at=0):
                self.at = at

            def __call__(self, *dims):
                n = int(np.prod(dims))
                v = work[:, self.at:self.at + n]
                self.at += n
                assert self.at <= WORK, self.at
                if len(dims) == 2:
                    v = v.rearrange("p (a b) -> p a b", b=dims[1])
                if len(dims) == 3:
                    v = v.rearrange("p (a b c) -> p a b c", b=dims[1], c=dims[2])
                return v

        def bc(ap, n):
            return ap.unsqueeze(2).to_broadcast([ap.shape[0], ap.shape[1], n])

        def bc1(ap, n):
            return ap.unsqueeze(1).to_broadcast([ap.shape[0], n, ap.shape[1]])

        arena = Arena(WORK - DC * T - 2 * T)
        squares, spread, rstd = arena(DC, T), arena(T), arena(T)

        def norm_pe(e, n):
            e.eng.wait_ge(S["tile_free"], e.c["tile"].at(-1))
            out_ = e.bank()
            for k in range(n):
                e.eng.wait_ge(S["squares"], e.c["squares"].next())
                ins = e.mm(out_, ones, squares[:, k, :], k == 0, k == n - 1)
            ins.then_inc(S["tile_done"], 1)

        def norm_act(e, src, n):
            for k in range(n):
                nc.scalar.activation(squares[:, k, :], src[:, k, :], ACT.Square).then_inc(S["squares"], 1)
            e.eng.wait_ge(S["tile_free"], e.c["tile"].next())
            nc.scalar.activation(spread, spread, ACT.Sqrt).then_inc(S["root"], 1)

        def norm_dve(e, src, dst, n, gain, width, eps):
            e.eng.wait_ge(S["tile_done"], e.c["tile"].next())
            t = e.result()
            nc.vector.tensor_scalar(spread, t, 1.0 / width, eps, ALU.mult, ALU.add).then_inc(S["tile_free"], 1)
            e.eng.wait_ge(S["tile_free"], e.c["tile"].at())
            e.eng.wait_ge(S["root"], e.c["root"].next())
            nc.vector.reciprocal(rstd, spread).then_inc(S["dve_chain"], 1)
            e.eng.wait_ge(S["dve_chain"], e.c["dve_chain"].next())
            for k in range(n):
                ins = nc.vector.scalar_tensor_tensor(out=dst[:, k, :], in0=src[:, k, :], scalar=gain[:, k:k + 1],
                                                     in1=rstd, op0=ALU.mult, op1=ALU.mult)
                if k < n - 1:
                    ins.then_inc(S["dve_chain"], 1)
                    e.eng.wait_ge(S["dve_chain"], e.c["dve_chain"].next())
            return ins

        def end(ins):
            ins.then_inc(S["stage"], 1)

        def row(first, n, at):
            return con[first:first + n, CON["ident"][0] + first + at:CON["ident"][0] + first + at + 1]\
                .to_broadcast([n, P])

        x_tok = Arena()(NB, D)
        N_INPUTS = 3

        def load_act(e):
            nc.scalar.dma_start(con[:, :], consts).then_inc(S["inputs"], 16)
            nc.scalar.dma_start(x_tok, x.rearrange("o (b p) d -> p (o b) d", p=P)).then_inc(S["inputs"], 16)
            nc.scalar.dma_start(vec[:, :], vecs).then_inc(S["inputs"], 16)
            e.eng.wait_ge(S["inputs"], 16 * N_INPUTS)

        def load_pe(e):
            e.eng.wait_ge(S["inputs"], 16 * N_INPUTS)
            for c in range(DC):
                if c >= 2:
                    e.eng.wait_ge(S["tile_free"], e.c["tile"].at(-1))
                o = e.bank()
                for b in range(NB):
                    ins = e.eng.transpose(o[:, P * b:P * b + P], x_tok[:, b, P * c:P * c + P], ident)
                ins.then_inc(S["tile_done"], 1)

        def load_dve(e):
            e.eng.wait_ge(S["inputs"], 16 * N_INPUTS)
            for c in range(DC):
                e.eng.wait_ge(S["tile_done"], e.c["tile"].next())
                nc.vector.tensor_copy(xT[:, c, :], e.result()).then_inc(S["tile_free"], 1)
                e.eng.wait_ge(S["tile_free"], e.c["tile"].at())
            e.tick()

        class Soft:

            def __init__(self, a):
                self.s, self.pr, self.pt = a(2, 768), a(2, 768), a(2, 768)
                self.mx, self.neg, self.den, self.inv = a(2, 1), a(2, 1), a(2, 1), a(2, 1)

        def turned_by_act(w):
            return {6: 4, 4: 2, 3: 2, 2: 1, 1: 1}[w // P]

        def unit_scores(e, u, products):
            for lo, w, q, k in products:
                ins = e.mm(flat[:, 1024 * (u % 2) + lo:1024 * (u % 2) + lo + w], q, k)
            ins.then_inc(S["scores"], 1)

        def unit_pe(e, A, units):
            unit_scores(e, 0, units[0][1])
            unit_scores(e, 1, units[1][1])
            for u, (w, _, values) in enumerate(units):
                e.eng.wait_ge(S["probs"], e.c["probs"].next())
                for b in range(w // P):
                    at = 2048 + P * b if b < turned_by_act(w) else 2560 + P * (b - turned_by_act(w))
                    ins = e.eng.transpose(flat[:, at:at + P], A.pr[:, u % 2, P * b:P * b + P], ident)
                ins.then_inc(S["turned"], 1)
                if u + 2 < len(units):
                    unit_scores(e, u + 2, units[u + 2][1])
                e.eng.wait_ge(S["turned_a"], e.c["turned_a"].next())
                e.eng.wait_ge(S["turned_b"], e.c["turned_b"].next())
                if u >= 2:
                    e.eng.wait_ge(S["unit_out"], e.c["unit_out"].next())
                o = acc[:, u % 2, 0:64]
                for b in range(w // P):
                    ins = e.mm(o, A.pt[:, u % 2, P * b:P * b + P], values[b], b == 0, b == w // P - 1)
                ins.then_inc(S["mixed"], 1)
            e.eng.wait_ge(S["unit_out"], e.c["unit_out"].next())
            e.eng.wait_ge(S["unit_out"], e.c["unit_out"].next())

        def unit_act(e, A, widths):
            def exps(u):
                w = widths[u]
                e.eng.wait_ge(S["maxima"], e.c["maxima"].next())
                nc.scalar.activation(A.pr[:, u % 2, 0:w], A.s[:, u % 2, 0:w], ACT.Exp, bias=A.neg[:, u % 2, :],
                                     accum_out=A.den[:, u % 2, :]).then_inc(S["probs"], 1)
            exps(0)
            exps(1)
            for u, w in enumerate(widths):
                e.eng.wait_ge(S["turned"], e.c["turned"].next())
                n = P * turned_by_act(w)
                nc.scalar.activation(A.pt[:, u % 2, 0:n], flat[:, 2048:2048 + n], ACT.Copy)\
                    .then_inc(S["turned_a"], 1)
                if u + 2 < len(widths):
                    exps(u + 2)

        def unit_dve(e, A, widths, masks, scale, outs):
            def maxima(u):
                w, d = widths[u], u % 2
                e.eng.wait_ge(S["scores"], e.c["scores"].next())
                nc.vector.memset(e.ticks, 0.0)
                nc.vector.tensor_tensor_reduce(
             out=A.s[:, d, 0:w], in0=flat[:, 1024 * d:1024 * d + w], in1=masks[u], scale=scale,
             scalar=-3.0e38, op0=ALU.add, op1=ALU.max, accum_out=A.mx[:, d, :]).then_inc(S["dve_chain"], 1)
                e.eng.wait_ge(S["dve_chain"], e.c["dve_chain"].next())
                nc.vector.tensor_scalar(A.neg[:, d, :], A.mx[:, d, :], -1.0, None, ALU.mult).then_inc(S["maxima"], 1)
            maxima(0)
            maxima(1)
            for u, w in enumerate(widths):
                e.eng.wait_ge(S["turned"], e.c["turned"].next())
                n = P * turned_by_act(w)
                if n < w:
                    ins = nc.vector.tensor_copy(A.pt[:, u % 2, n:w], flat[:, 2560:2560 + w - n])
                else:
                    ins = nc.vector.memset(e.ticks, 0.0)
                ins.then_inc(S["turned_b"], 1)
                nc.vector.reciprocal(A.inv[:, u % 2, :], A.den[:, u % 2, :]).then_inc(S["dve_chain"], 1)
                e.eng.wait_ge(S["dve_chain"], e.c["dve_chain"].next())
                if u + 2 < len(widths):
                    maxima(u + 2)
                e.eng.wait_ge(S["mixed"], e.c["mixed"].next())
                nc.vector.tensor_scalar(outs[u], acc[:, u % 2, 0:64], A.inv[:, u % 2, :], None, ALU.mult)\
                    .then_inc(S["unit_out"], 1)

        def tokens_to_features_pe(e, tok, strided):
            for c in range(4):
                e.eng.wait_ge(S["tile_free"], e.c["tile"].at(-1))
                o = e.bank()
                for b in range(NB):
                    ins = e.eng.transpose(o[:, P * b:P * b + P], tok[:, b, P * c:P * c + P], ident)
                ins.then_inc(S["tile_done"], 1)

        def tokens_to_features_dve(e, dst, strided):
            for c in range(4):
                e.eng.wait_ge(S["tile_done"], e.c["tile"].next())
                t = e.result()
                if strided:
                    t = t.rearrange("p (b u) -> p b u", b=NB)
                    d = dst[:, c, :].rearrange("p (u b) -> p b u", b=NB)
                else:
                    d = dst[:, c, :]
                nc.vector.tensor_copy(d, t).then_inc(S["tile_free"], 1)
                e.eng.wait_ge(S["tile_free"], e.c["tile"].at())

        a = Arena()
        va = a(GROUPS, NB, 512)
        o_tok = a(NB, 512)
        qk = a(6, T)
        qk_sq = a(6, T)
        q_one = a(2, GROUPS, T)
        AS = Soft(a)

        def tokens_of(g, b, ap):
            return ap[:, P * b:P * b + P] if g == 0 else ap[:, b::4]

        def values_pe(e):
            for g in range(GROUPS):
                if g:
                    e.eng.wait_ge(S["values_out"], e.c["values_out"].next())
                for k in range(DC):
                    if k % 4 == 0:
                        e.eng.wait_ge(S[e.landing()], e.landed())
                        w = e.slot(ring)
                    for b in range(NB):
                        ins = e.mm(bank[:, b, :], tokens_of(g, b, hT[:, k, :]), w[:, 512 * (k % 4):512 * (k % 4) + 512],
                                   k == 0, k == DC - 1)
                ins.then_inc(S["values"], 1)

        def values_dve(e):
            for g in range(GROUPS):
                e.eng.wait_ge(S["values"], e.c["values"].next())
                for b in range(NB):
                    ins = nc.vector.tensor_copy(va[:, g, b, :], bank[:, b, :])
                    if b < NB - 1:
                        ins.then_inc(S["dve_chain"], 1)
                        e.eng.wait_ge(S["dve_chain"], e.c["dve_chain"].next())
                ins.then_inc(S["values_out"], 1)

        def attn_units(p_):
            units = []
            for hh in range(2):
                for r in range(NB):
                    prods = [(0, 512, q_one[:, hh, 0, r::4], qk[:, 1, :])]
                    for g in (1, 2):
                        prods.append((512 + P * (g - 1), P, q_one[:, hh, g, r::4], qk[:, 2 * g + 1, r::4]))
                    cols = bass.ds(p_ * P + 64 * hh, 64)
                    vals = [va[:, 0, b, cols] for b in range(4)] + [va[:, g, r, cols] for g in (1, 2)]
                    units.append((768, prods, vals))
            return units

        def attn_pe(e):
            with loop(e, 4, fill=4, tile=12, squares=6, qk_ready=1, probs=8, turned_a=8, turned_b=8, unit_out=8) as p_:
                for j in range(6 + 1):
                    if j < 6:
                        if j % 2 == 0:
                            e.eng.wait_ge(S[e.landing()], e.landed())
                            w = e.slot(ring)
                        e.eng.wait_ge(S["tile_free"], e.c["tile"].at(-1))
                        e.dense(e.bank(), blocks(w, 8 * (j % 2), 8), [hT[:, k, :] for k in range(DC)])
                    if j == 6:
                        e.eng.wait_ge(S[e.landing()], e.landed())
                        e.slot(ring)
                    if j >= 1:
                        e.eng.wait_ge(S["tile_free"], e.c["tile"].at(-1))
                        o = e.bank()
                        e.eng.wait_ge(S["squares"], e.c["squares"].next())
                        e.mm(o[:, 0:256], pair_ones, qk_sq[:, j - 1, 0:256])
                        e.mm(o[:, 256:512], pair_ones, qk_sq[:, j - 1, 256:512]).then_inc(S["tile_done"], 1)
                e.eng.wait_ge(S["qk_ready"], e.c["qk_ready"].next())
                unit_pe(e, AS, attn_units(p_))
            tokens_to_features_pe(e, o_tok, True)

        def attn_act(e):
            with loop(e, 4, tile=12, maxima=8, turned=8):
                for j in range(6 + 1):
                    if j < 6:
                        e.eng.wait_ge(S["tile_free"], e.c["tile"].next())
                        nc.scalar.activation(qk_sq[:, j, :], qk[:, j, :], ACT.Square).then_inc(S["squares"], 1)
                    if j >= 1:
                        e.eng.wait_ge(S["tile_free"], e.c["tile"].next())
                        nc.scalar.activation(qk_sq[:, j - 1, :], qk_sq[:, j - 1, :], ACT.Sqrt).then_inc(S["root"], 1)
                unit_act(e, AS, [768] * 8)
            e.skip(4)

        def attn_dve(e):
            masks = C("attn_mask").rearrange("p (r n) -> p r n", r=NB)
            nc.vector.memset(q_one[64:P, 0, :, :], 0.0).then_inc(S["dve_chain"], 1)
            e.eng.wait_ge(S["dve_chain"], e.c["dve_chain"].next())
            nc.vector.memset(q_one[0:64, 1, :, :], 0.0).then_inc(S["dve_chain"], 1)
            e.eng.wait_ge(S["dve_chain"], e.c["dve_chain"].next())
            with loop(e, 4, tile=12, root=6, scores=8, turned=8, mixed=8, dve_chain=27) as p_:
                def scaled(j):
                    e.eng.wait_ge(S["root"], e.c["root"].next())
                    nc.vector.reciprocal(qk_sq[:, j, :], qk_sq[:, j, :]).then_inc(S["dve_chain"], 1)
                    e.eng.wait_ge(S["dve_chain"], e.c["dve_chain"].next())
                    if j % 2 == 0:
                        for hh in range(2):
                            r = slice(64 * hh, 64 * hh + 64)
                            ins = nc.vector.scalar_tensor_tensor(
                                out=q_one[r, hh, j // 2, :], in0=qk[r, j, :], scalar=V("q_norm")[r, :],
                                in1=qk_sq[r, j, :], op0=ALU.mult, op1=ALU.mult)
                        return ins
                    return nc.vector.scalar_tensor_tensor(
                        out=qk[:, j, :], in0=qk[:, j, :], scalar=V("k_norm"),
                        in1=qk_sq[:, j, :], op0=ALU.mult, op1=ALU.mult)

                for j in range(6 + 1):
                    if j < 6:
                        e.eng.wait_ge(S["tile_done"], e.c["tile"].next())
                        nc.vector.tensor_copy(qk[:, j, :], e.result()).then_inc(S["tile_free"], 1)
                        e.eng.wait_ge(S["tile_free"], e.c["tile"].at())
                    if j >= 2:
                        scaled(j - 2).then_inc(S["dve_chain"], 1)
                        e.eng.wait_ge(S["dve_chain"], e.c["dve_chain"].next())
                    if j >= 1:
                        e.eng.wait_ge(S["tile_done"], e.c["tile"].next())
                        nc.vector.tensor_scalar(qk_sq[:, j - 1, :], e.result(), 1.0 / AD, EPS, ALU.mult, ALU.add)\
                            .then_inc(S["tile_free"], 1)
                        e.eng.wait_ge(S["tile_free"], e.c["tile"].at())
                ins = scaled(5)
                ins.then_inc(S["qk_ready"], 1)
                outs = [o_tok[:, r, bass.ds(p_ * P + 64 * hh, 64)] for hh in range(2) for r in range(NB)]
                unit_dve(e, AS, [768] * 8, [masks[:, r, :] for _ in range(2) for r in range(NB)], AD ** -0.5, outs)
            tokens_to_features_dve(e, mixT, True)
            e.tick()

        a = Arena()
        gcum_rows, beta_rows = a(DH, T), a(DH, T)
        cols = a(NB, P)
        e_cols = a(3, NB, 8)
        loop_at = a.at
        rows = a(T)
        al, mneg, sp, gdec = a(T), a(T), a(T), a(T)
        ea, rawb = a(1), a(T)

        def decay_pe(e):
            e.eng.wait_ge(S[e.landing()], e.landed())
            w = e.slot(ring)
            for half in range(2):
                e.eng.wait_ge(S["tile_free"], e.c["tile"].at(-1))
                e.dense(e.bank()[0:8, :], blocks(w, 8 * half, 8, 8), [hT[:, k, :] for k in range(DC)])
            e.eng.wait_ge(S["rows"], e.c["rows"].next())
            for h in range(DH):
                e.eng.wait_ge(S["tile_free"], e.c["tile"].at(-1))
                e.mm(e.bank(), row(0, 8, h), rows[0:8, :]).then_inc(S["tile_done"], 1)
                e.eng.wait_ge(S["tile_free"], e.c["tile"].at(-1))
                e.mm(e.bank(), row(32, 8, h), rows[32:40, :]).then_inc(S["tile_done"], 1)
            e.eng.wait_ge(S["tile_free"], e.c["tile"].at(-1))
            o = e.bank()
            for b in range(NB):
                ins = e.eng.transpose(o[:, P * b:P * b + P], rows[:, P * b:P * b + P], ident)
            ins.then_inc(S["tile_done"], 1)

        def decay_act(e):
            e.eng.wait_ge(S["tile_free"], e.c["tile"].next())
            nc.scalar.activation(rows[32:40, :], rawb[0:8, :], ACT.Sigmoid).then_inc(S["beta"], 1)
            e.eng.wait_ge(S["minus_abs"], e.c["minus_abs"].next())
            nc.scalar.activation(ea[0:8, :], V("a_log")[0:8, :], ACT.Exp).then_inc(S["rate"], 1)
            nc.scalar.activation(mneg[0:8, :], mneg[0:8, :], ACT.Exp).then_inc(S["act_chain"], 1)
            e.eng.wait_ge(S["act_chain"], e.c["act_chain"].next())
            nc.scalar.activation(mneg[0:8, :], mneg[0:8, :], ACT.Ln, bias=1.0).then_inc(S["log1p"], 1)
            e.skip(1 + 16)
            e.eng.wait_ge(S["tile_free"], e.c["tile"].next())
            nc.scalar.activation(e_cols[:, 0, :, :], cols[:, :, 64:72], ACT.Exp)
            nc.scalar.activation(e_cols[:, 1, :, :], cols[:, :, 0:8], ACT.Exp).then_inc(S["col_exp"], 1)

        def decay_dve(e):
            nc.vector.memset(rows, 0.0).then_inc(S["dve_chain"], 1)
            e.eng.wait_ge(S["dve_chain"], e.c["dve_chain"].next())
            e.eng.wait_ge(S["tile_done"], e.c["tile"].next())
            nc.vector.tensor_copy(rawb[0:8, :], e.result()[0:8, :]).then_inc(S["tile_free"], 1)
            e.eng.wait_ge(S["tile_free"], e.c["tile"].at())
            e.eng.wait_ge(S["tile_done"], e.c["tile"].next())
            nc.vector.tensor_scalar(al[0:8, :], e.result()[0:8, :], V("dt_bias")[0:8, :], None, ALU.add)\
                .then_inc(S["tile_free"], 1)
            e.eng.wait_ge(S["tile_free"], e.c["tile"].at())
            nc.vector.tensor_scalar(sp[0:8, :], al[0:8, :], 0.0, None, ALU.max).then_inc(S["dve_chain"], 1)
            e.eng.wait_ge(S["dve_chain"], e.c["dve_chain"].next())
            nc.vector.scalar_tensor_tensor(out=mneg[0:8, :], in0=sp[0:8, :], scalar=-2.0, in1=al[0:8, :],
                                           op0=ALU.mult, op1=ALU.add).then_inc(S["minus_abs"], 1)
            e.eng.wait_ge(S["rate"], e.c["rate"].next())
            e.eng.wait_ge(S["log1p"], e.c["log1p"].next())
            nc.vector.tensor_tensor(sp[0:8, :], sp[0:8, :], mneg[0:8, :], ALU.add).then_inc(S["dve_chain"], 1)
            e.eng.wait_ge(S["dve_chain"], e.c["dve_chain"].next())
            nc.vector.tensor_scalar(gdec[0:8, :], sp[0:8, :], ea[0:8, :], -1.0, ALU.mult, ALU.mult)\
                .then_inc(S["dve_chain"], 1)
            e.eng.wait_ge(S["dve_chain"], e.c["dve_chain"].next())
            nc.vector.tensor_tensor_scan(rows[0:8, :], C("not_start")[0:8, :], gdec[0:8, :], 0.0,
                                         ALU.mult, ALU.add).then_inc(S["dve_chain"], 1)
            e.eng.wait_ge(S["dve_chain"], e.c["dve_chain"].next())
            g3 = rows[0:8, :].rearrange("p (c i) -> p c i", i=CH)
            nc.vector.tensor_copy(al[0:8, 0:8], g3[:, :, CH - 1]).then_inc(S["dve_chain"], 1)
            e.eng.wait_ge(S["dve_chain"], e.c["dve_chain"].next())
            e.eng.wait_ge(S["beta"], e.c["beta"].next())
            nc.vector.tensor_tensor(rows[64:72, :].rearrange("p (c i) -> p c i", i=CH), bc(al[0:8, 0:8], CH), g3,
                                    ALU.subtract).then_inc(S["rows"], 1)
            for h in range(DH):
                e.eng.wait_ge(S["tile_done"], e.c["tile"].next())
                nc.vector.tensor_copy(gcum_rows[:, h, :], e.result()).then_inc(S["tile_free"], 1)
                e.eng.wait_ge(S["tile_free"], e.c["tile"].at())
                e.eng.wait_ge(S["tile_done"], e.c["tile"].next())
                nc.vector.tensor_copy(beta_rows[:, h, :], e.result()).then_inc(S["tile_free"], 1)
                e.eng.wait_ge(S["tile_free"], e.c["tile"].at())
            e.eng.wait_ge(S["tile_done"], e.c["tile"].next())
            nc.vector.tensor_copy(cols, e.result().rearrange("p (b n) -> p b n", b=NB)).then_inc(S["tile_free"], 1)
            e.eng.wait_ge(S["tile_free"], e.c["tile"].at())
            e.eng.wait_ge(S["col_exp"], e.c["col_exp"].next())
            nc.vector.tensor_tensor(e_cols[:, 1, :, :], e_cols[:, 1, :, :], cols[:, :, 32:40], ALU.mult)\
                .then_inc(S["dve_chain"], 1)
            e.eng.wait_ge(S["dve_chain"], e.c["dve_chain"].next())
            nc.vector.tensor_copy(e_cols[:, 2, :, :], cols[:, :, 32:40])
            e.tick()

        a = Arena(loop_at)
        spare = [C("attn_mask")[:, T * n:T * n + T] for n in range(6)]

        class Head:

            def __init__(self, s):
                self.pad = a(3, 3 + T)
                self.qkv = a(3, T)
                self.zs, self.sq, self.kbT, self.dec = a(T), a(2, T), a(T), a(T)
                self.eg, self.qdT, self.attnT = spare[3 * s:3 * s + 3]
                self.hc, self.gcol, self.taps, self.state = a(3, NB), a(NB), a(3, 4), a(P)
                self.vnew = a(2, P)
                self.qT, self.kT, self.vT = (self.qkv[:, j, :] for j in range(3))
                self.k_tail, self.k_bg, self.v_b = (self.pad[:, j, 3:3 + T] for j in range(3))
                self.aT, self.xinvT, self.xinv, self.prod = self.kbT, self.qT, self.kT, self.vT
                self.level, self.wT, self.u = self.sq[:, 1, :], self.sq[:, 0, :], self.dec
                self.raw, self.osq = self.aT, self.level
                self.root, self.inv = self.prod, self.xinv
                self.bank0 = 3 * s

        H = [Head(0), Head(1)]

        def blk(ap, b):
            return ap[:, P * b:P * b + P]

        def by_block(ap):
            return ap.rearrange("p (b n) -> p b n", b=NB)

        def dyn(ap, n):
            return ap[:, bass.ds(n, 1), :].rearrange("p o n -> p (o n)")

        def per_block(e, products):
            e.eng.wait_ge(S["tile_free"], e.c["tile"].at(-1))
            o = e.bank()
            for b in range(NB):
                ins = e.mm(blk(o, b), *products(b))
            ins.then_inc(S["tile_done"], 1)

        def delta_pe(e):
            for h in H:
                for _ in range(2):
                    e.eng.wait_ge(S[e.landing()], e.landed())
                    w = e.slot(ring)
                    for half in range(2):
                        e.eng.wait_ge(S["tile_free"], e.c["tile"].at(-1))
                        e.dense(e.bank(), blocks(w, 8 * half, 8), [hT[:, k, :] for k in range(DC)])
            for h in H:
                for j in range(2):
                    e.eng.wait_ge(S["tile_free"], e.c["tile"].at(-1))
                    o = e.bank()
                    e.eng.wait_ge(S["squares"], e.c["squares"].next())
                    e.mm(o, ones, h.sq[:, j, :]).then_inc(S["tile_done"], 1)
            for h in H:
                e.eng.wait_ge(S["kq_ready"], e.c["kq_ready"].next())
                for src in (h.kT, h.vT):
                    e.eng.wait_ge(S["tile_free"], e.c["tile"].at(-1))
                    o = e.bank()
                    for b in range(NB):
                        ins = e.eng.transpose(blk(o, b), blk(src, b), ident)
                    ins.then_inc(S["tile_done"], 1)
            for h in H:
                per_block(e, lambda b: (blk(h.kT, b), blk(h.kbT, b)))
                per_block(e, lambda b: (blk(h.kT, b), blk(h.qT, b)))
            for n in range(6):
                if n == 0:
                    for h in H:
                        e.eng.wait_ge(S["level"], e.c["level"].next())
                        per_block(e, lambda b: (blk(h.level, b), ident))
                    continue
                for h in H:
                    e.eng.wait_ge(S["level"], e.c["level"].next())
                    per_block(e, lambda b: (blk(h.level, b), blk(h.xinv, b)))
                for s, h in enumerate(H):
                    if s == 0:
                        e.eng.wait_ge(S["tile_free"], e.c["tile"].at(-1))
                    else:
                        e.eng.wait_ge(S["tile_free"], e.c["tile"].at(-2 if n < 5 else -1))
                    if n < 5:
                        per_block(e, lambda b: (blk(h.xinvT, b), blk(h.prod, b)))
                    per_block(e, lambda b: (blk(h.prod, b), blk(h.xinvT, b)))
            for h in H:
                e.eng.wait_ge(S["inverse"], e.c["inverse"].next())
                per_block(e, lambda b: (blk(h.xinvT, b), blk(h.v_b, b)))
                per_block(e, lambda b: (blk(h.k_bg, b), blk(h.xinvT, b)))
            for c in range(T // CH):
                b, lo = c // 2, (c % 2) * CH
                r = slice(lo, lo + CH)
                for h in H:
                    e.eng.wait_ge(S["state"], e.c["state"].next())
                    e.mm(bank[:, h.bank0, 0:P], blk(h.wT, b), h.state).then_inc(S["w_state"], 1)
                    e.mm(bank[:, h.bank0 + 2, CH * c:CH * c + CH], h.state, h.qdT[:, CH * c:CH * c + CH], True, False)
                for h in H:
                    e.eng.wait_ge(S["vnew"], e.c["vnew"].next())
                    v = h.vnew[:, c % 2, :]
                    e.mm(bank[:, h.bank0 + 1, 0:P], blk(h.k_tail, b), v).then_inc(S["k_vnew"], 1)
                    ins = e.mm(bank[:, h.bank0 + 2, CH * c:CH * c + CH], v, blk(h.attnT, b)[:, r], False, True)
                    if c == T // CH - 1:
                        ins.then_inc(S["delta_out"], 1)
            for h in H:
                e.eng.wait_ge(S["tile_free"], e.c["tile"].at(-1))
                o = e.bank()
                e.eng.wait_ge(S["squares"], e.c["squares"].next())
                e.mm(o, ones, h.osq).then_inc(S["tile_done"], 1)

        def delta_act(e, hd):
            def after_filter(h, j):
                e.eng.wait_ge(S["filtered"], e.c["filtered"].next())
                nc.scalar.activation(h.qkv[:, j, :], h.qkv[:, j, :], ACT.Silu).then_inc(S["act_chain"], 1)
                e.eng.wait_ge(S["act_chain"], e.c["act_chain"].next())
                if j < 2:
                    nc.scalar.activation(h.sq[:, j, :], h.qkv[:, j, :], ACT.Square).then_inc(S["squares"], 1)

            for s, h in enumerate(H):
                e.eng.wait_ge(S["pad_free"], e.c["pad_free"].next())
                for j in range(3):
                    e.eng.wait_ge(S["tile_done"], e.c["tile"].next())
                    t = e.result()
                    e.eng.wait_ge(S["tile_free"], e.c["tile"].at(-1))
                    nc.scalar.activation(h.pad[:, j, 3:3 + T], t, ACT.Copy).then_inc(S["tile_free"], 1)
                    e.eng.wait_ge(S["tile_free"], e.c["tile"].at())
                    if j > 0:
                        after_filter(h, j - 1)
                e.eng.wait_ge(S["tile_done"], e.c["tile"].next())
                t = e.result()
                e.eng.wait_ge(S["tile_free"], e.c["tile"].at(-1))
                nc.scalar.activation(h.zs, t, ACT.Silu).then_inc(S["tile_free"], 1)
                e.eng.wait_ge(S["tile_free"], e.c["tile"].at())
                after_filter(h, 2)
            for s, h in enumerate(H):
                nc.scalar.activation(h.eg, dyn(gcum_rows, hd(s)), ACT.Exp).then_inc(S["exp_rows"], 1)
                e.eng.wait_ge(S["decay_arg"], e.c["decay_arg"].next())
                nc.scalar.activation(h.dec, h.dec, ACT.Exp).then_inc(S["decay"], 1)
            for h in H:
                e.skip(1)
                e.eng.wait_ge(S["tile_free"], e.c["tile"].next())
                nc.scalar.activation(h.sq, h.sq, ACT.Sqrt).then_inc(S["root"], 1)
            e.skip(2 * (2 + 2 + 1))
            for n in range(1, 6):
                for h in H:
                    e.eng.wait_ge(S["tile_done"], e.c["tile"].next())
                    t = e.result()
                    e.eng.wait_ge(S["tile_free"], e.c["tile"].at(-1))
                    nc.scalar.activation(h.prod, t, ACT.Copy).then_inc(S["tile_free"], 1)
                    e.eng.wait_ge(S["tile_free"], e.c["tile"].at())
                e.skip(4 if n < 5 else 2)
            for h in H:
                for dst in (h.u, h.wT):
                    e.eng.wait_ge(S["tile_done"], e.c["tile"].next())
                    t = e.result()
                    e.eng.wait_ge(S["tile_free"], e.c["tile"].at(-1))
                    nc.scalar.activation(dst, t, ACT.Copy).then_inc(S["tile_free"], 1)
                    e.eng.wait_ge(S["tile_free"], e.c["tile"].at())
            for h in H:
                e.eng.wait_ge(S["delta_raw"], e.c["delta_raw"].next())
                nc.scalar.activation(h.osq, h.raw, ACT.Square).then_inc(S["squares"], 1)
            for h in H:
                e.eng.wait_ge(S["tile_free"], e.c["tile"].next())
                nc.scalar.activation(h.root, h.root, ACT.Sqrt).then_inc(S["root"], 1)

        def delta_dve(e, hd):
            for s, h in enumerate(H):
                for j in range(3):
                    nc.vector.tensor_copy(h.taps[:, j, :].unsqueeze(1), V("conv_w").rearrange(
                 "p (n t) -> p n t", t=4)[:, bass.ds(hd(s) + 8 * j, 1), :]).then_inc(S["dve_chain"], 1)
                    e.eng.wait_ge(S["dve_chain"], e.c["dve_chain"].next())
                nc.vector.tensor_copy(h.gcol.unsqueeze(2), cols[:, :, bass.ds(hd(s), 1)]).then_inc(S["dve_chain"], 1)
                e.eng.wait_ge(S["dve_chain"], e.c["dve_chain"].next())
                for j in range(3):
                    nc.vector.tensor_copy(h.hc[:, j, :].unsqueeze(2), e_cols[:, j, :, bass.ds(hd(s), 1)])\
                        .then_inc(S["dve_chain"], 1)
                    e.eng.wait_ge(S["dve_chain"], e.c["dve_chain"].next())
                nc.vector.memset(e.ticks, 0.0).then_inc(S["pad_free"], 1)
                for j in range(3):
                    e.eng.wait_ge(S["tile_free"], e.c["tile"].next())
                    y = h.qkv[:, j, :]
                    nc.vector.tensor_scalar(y, h.pad[:, j, 3:3 + T], h.taps[:, j, 3:4], None, ALU.mult)\
                        .then_inc(S["dve_chain"], 1)
                    e.eng.wait_ge(S["dve_chain"], e.c["dve_chain"].next())
                    for t in range(3):
                        ins = nc.vector.scalar_tensor_tensor(out=y, in0=h.pad[:, j, t:t + T],
                                                             scalar=h.taps[:, j, t:t + 1],
                                                             in1=y, op0=ALU.mult, op1=ALU.add)
                        if t < 2:
                            ins.then_inc(S["dve_chain"], 1)
                            e.eng.wait_ge(S["dve_chain"], e.c["dve_chain"].next())
                    ins.then_inc(S["filtered"], 1)
                e.eng.wait_ge(S["tile_free"], e.c["tile"].next())
                nc.vector.tensor_tensor(by_block(h.dec), by_block(dyn(gcum_rows, hd(s))), bc(h.gcol, P),
                                        ALU.subtract).then_inc(S["dve_chain"], 1)
                e.eng.wait_ge(S["dve_chain"], e.c["dve_chain"].next())
                nc.vector.tensor_tensor(by_block(h.dec), by_block(h.dec), bc1(C("decay_mask"), NB), ALU.add)\
                    .then_inc(S["decay_arg"], 1)
            for h in H:
                for j in range(2):
                    e.eng.wait_ge(S["tile_done"], e.c["tile"].next())
                    nc.vector.tensor_scalar(h.sq[:, j, :], e.result(), EPS, None, ALU.add).then_inc(S["tile_free"], 1)
                    e.eng.wait_ge(S["tile_free"], e.c["tile"].at())
            for s, h in enumerate(H):
                e.eng.wait_ge(S["root"], e.c["root"].next())
                nc.vector.reciprocal(h.sq, h.sq).then_inc(S["dve_chain"], 1)
                e.eng.wait_ge(S["dve_chain"], e.c["dve_chain"].next())
                nc.vector.scalar_tensor_tensor(out=h.qT, in0=h.qT, scalar=DD ** -0.5, in1=h.sq[:, 0, :],
                                               op0=ALU.mult, op1=ALU.mult).then_inc(S["dve_chain"], 1)
                e.eng.wait_ge(S["dve_chain"], e.c["dve_chain"].next())
                nc.vector.tensor_tensor(h.kT, h.kT, h.sq[:, 1, :], ALU.mult).then_inc(S["dve_chain"], 1)
                e.eng.wait_ge(S["dve_chain"], e.c["dve_chain"].next())
                nc.vector.tensor_tensor(h.kbT, h.kT, dyn(beta_rows, hd(s)), ALU.mult).then_inc(S["kq_ready"], 1)
            for h in H:
                e.eng.wait_ge(S["exp_rows"], e.c["exp_rows"].next())
                nc.vector.tensor_tensor(h.qdT, h.qT, h.eg, ALU.mult).then_inc(S["dve_chain"], 1)
                e.eng.wait_ge(S["dve_chain"], e.c["dve_chain"].next())
                e.eng.wait_ge(S["tile_done"], e.c["tile"].next())
                t = by_block(e.result())
                nc.vector.tensor_tensor(by_block(h.k_tail), t, bc(h.hc[:, 0, :], P), ALU.mult).then_inc(S["dve_chain"], 1)
                e.eng.wait_ge(S["dve_chain"], e.c["dve_chain"].next())
                nc.vector.tensor_tensor(by_block(h.k_bg), t, bc(h.hc[:, 1, :], P), ALU.mult).then_inc(S["tile_free"], 1)
                e.eng.wait_ge(S["tile_free"], e.c["tile"].at())
                e.eng.wait_ge(S["tile_done"], e.c["tile"].next())
                nc.vector.tensor_tensor(by_block(h.v_b), by_block(e.result()), bc(h.hc[:, 2, :], P), ALU.mult)\
                    .then_inc(S["tile_free"], 1)
                e.eng.wait_ge(S["tile_free"], e.c["tile"].at())
            for h in H:
                e.eng.wait_ge(S["decay"], e.c["decay"].next())
                e.eng.wait_ge(S["tile_done"], e.c["tile"].next())
                nc.vector.tensor_tensor(h.aT, e.result(), h.dec, ALU.mult).then_inc(S["tile_free"], 1)
                e.eng.wait_ge(S["tile_free"], e.c["tile"].at())
                e.eng.wait_ge(S["tile_done"], e.c["tile"].next())
                nc.vector.tensor_tensor(h.attnT, e.result(), h.dec, ALU.mult).then_inc(S["tile_free"], 1)
                e.eng.wait_ge(S["tile_free"], e.c["tile"].at())
            for h in H:
                nc.vector.tensor_tensor(by_block(h.aT), by_block(h.aT), bc1(C("strict"), NB), ALU.mult)\
                    .then_inc(S["dve_chain"], 1)
                e.eng.wait_ge(S["dve_chain"], e.c["dve_chain"].next())
            for n in range(6):
                lv = C("level")[:, P * n:P * n + P]
                for h in H:
                    nc.vector.tensor_tensor(by_block(h.level), by_block(h.aT), bc1(lv, NB), ALU.mult)\
                        .then_inc(S["level"], 1)
                    e.eng.wait_ge(S["level"], e.c["level"].next())
                if n == 0:
                    for h in H:
                        nc.vector.tensor_tensor(by_block(h.xinvT), bc1(ident, NB), by_block(h.level), ALU.subtract)\
                            .then_inc(S["dve_chain"], 1)
                        e.eng.wait_ge(S["dve_chain"], e.c["dve_chain"].next())
                        e.eng.wait_ge(S["tile_done"], e.c["tile"].next())
                        nc.vector.tensor_tensor(by_block(h.xinv), bc1(ident, NB), by_block(e.result()), ALU.subtract)\
                            .then_inc(S["tile_free"], 1)
                        e.eng.wait_ge(S["tile_free"], e.c["tile"].at())
                    continue
                for h in H:
                    e.eng.wait_ge(S["tile_free"], e.c["tile"].next())
                for h in H:
                    if n < 5:
                        e.eng.wait_ge(S["tile_done"], e.c["tile"].next())
                        nc.vector.tensor_tensor(h.xinv, h.xinv, e.result(), ALU.subtract).then_inc(S["tile_free"], 1)
                        e.eng.wait_ge(S["tile_free"], e.c["tile"].at())
                    e.eng.wait_ge(S["tile_done"], e.c["tile"].next())
                    nc.vector.tensor_tensor(h.xinvT, h.xinvT, e.result(), ALU.subtract).then_inc(S["tile_free"], 1)
                    e.eng.wait_ge(S["tile_free"], e.c["tile"].at())
                    if n == 5:
                        nc.vector.memset(e.ticks, 0.0).then_inc(S["inverse"], 1)
            for h in H:
                e.eng.wait_ge(S["tile_free"], e.c["tile"].next())
                e.eng.wait_ge(S["tile_free"], e.c["tile"].next())
                nc.vector.memset(h.state, 0.0).then_inc(S["state"], 1)
                e.eng.wait_ge(S["state"], e.c["state"].next())
            for c in range(T // CH):
                b, lo = c // 2, (c % 2) * CH
                r = slice(lo, lo + CH)
                for h in H:
                    e.eng.wait_ge(S["w_state"], e.c["w_state"].next())
                    nc.vector.tensor_tensor(h.vnew[r, c % 2, :], blk(h.u, b)[r, :], bank[r, h.bank0, 0:P], ALU.subtract)\
                        .then_inc(S["vnew"], 1)
                for h in H:
                    e.eng.wait_ge(S["k_vnew"], e.c["k_vnew"].next())
                    ins = nc.vector.scalar_tensor_tensor(out=h.state, in0=h.state,
                                                         scalar=h.eg[:, CH * c + CH - 1:CH * c + CH],
                                                         in1=bank[:, h.bank0 + 1, 0:P], op0=ALU.mult, op1=ALU.add)
                    if c < T // CH - 1:
                        ins.then_inc(S["state"], 1)
                        e.eng.wait_ge(S["state"], e.c["state"].next())
                    else:
                        ins.then_inc(S["dve_chain"], 1)
                        e.eng.wait_ge(S["dve_chain"], e.c["dve_chain"].next())
            for h in H:
                e.eng.wait_ge(S["delta_out"], e.c["delta_out"].next())
                nc.vector.tensor_copy(h.raw, bank[:, h.bank0 + 2, :]).then_inc(S["delta_raw"], 1)
                e.eng.wait_ge(S["delta_raw"], e.c["delta_raw"].next())
            for h in H:
                e.eng.wait_ge(S["tile_done"], e.c["tile"].next())
                nc.vector.tensor_scalar(h.root, e.result(), 1.0 / DD, EPS, ALU.mult, ALU.add).then_inc(S["tile_free"], 1)
                e.eng.wait_ge(S["tile_free"], e.c["tile"].at())
            for s, h in enumerate(H):
                e.eng.wait_ge(S["root"], e.c["root"].next())
                nc.vector.reciprocal(h.inv, h.root).then_inc(S["dve_chain"], 1)
                e.eng.wait_ge(S["dve_chain"], e.c["dve_chain"].next())
                nc.vector.scalar_tensor_tensor(out=h.inv, in0=h.raw, scalar=V("dn_out_norm"), in1=h.inv,
                                               op0=ALU.mult, op1=ALU.mult).then_inc(S["dve_chain"], 1)
                e.eng.wait_ge(S["dve_chain"], e.c["dve_chain"].next())
                nc.vector.tensor_tensor(mixT[:, bass.ds(4 + hd(s), 1), :], h.inv.unsqueeze(1),
                                        h.zs.unsqueeze(1), ALU.mult).then_inc(S["dve_chain"], 1)
                e.eng.wait_ge(S["dve_chain"], e.c["dve_chain"].next())

        a = Arena()
        ga, gb, t1, t2 = a(2, T), a(2, T), a(2, T), a(2, T)
        mergedT = a(DC, T)

        def merge_pe(e):
            with loop(e, 4, fill=4, tile=8):
                for _ in range(2):
                    e.eng.wait_ge(S[e.landing()], e.landed())
                    w = e.slot(ring)
                    for half in range(2):
                        e.eng.wait_ge(S["tile_free"], e.c["tile"].at(-1))
                        e.dense(e.bank(), blocks(w, 8 * half, 8), [hT[:, k, :] for k in range(DC)])
                    e.eng.wait_ge(S[e.landing()], e.landed())
                    w = e.slot(ring)
                    e.eng.wait_ge(S["tile_free"], e.c["tile"].at(-1))
                    e.dense(e.bank(), blocks(w, 0, 4), [mixT[:, k, :] for k in range(4)])
                    e.eng.wait_ge(S["tile_free"], e.c["tile"].at(-1))
                    e.dense(e.bank(), blocks(w, 4, 8), [mixT[:, 4 + k, :] for k in range(8)])

        def merge_act(e):
            with loop(e, 4, tile=8):
                for s in range(2):
                    for g in (ga, gb):
                        e.eng.wait_ge(S["tile_done"], e.c["tile"].next())
                        t = e.result()
                        e.eng.wait_ge(S["tile_free"], e.c["tile"].at(-1))
                        nc.scalar.activation(g[:, s, :], t, ACT.Sigmoid).then_inc(S["tile_free"], 1)
                        e.eng.wait_ge(S["tile_free"], e.c["tile"].at())
                    e.skip(2)

        def merge_dve(e):
            with loop(e, 4, tile=8, dve_chain=2) as i:
                for s in range(2):
                    e.eng.wait_ge(S["tile_free"], e.c["tile"].next())
                    e.eng.wait_ge(S["tile_free"], e.c["tile"].next())
                    e.eng.wait_ge(S["tile_done"], e.c["tile"].next())
                    nc.vector.tensor_tensor(t1[:, s, :], e.result(), ga[:, s, :], ALU.mult).then_inc(S["tile_free"], 1)
                    e.eng.wait_ge(S["tile_free"], e.c["tile"].at())
                    e.eng.wait_ge(S["tile_done"], e.c["tile"].next())
                    nc.vector.tensor_tensor(t2[:, s, :], e.result(), gb[:, s, :], ALU.mult).then_inc(S["tile_free"], 1)
                    e.eng.wait_ge(S["tile_free"], e.c["tile"].at())
                    nc.vector.tensor_tensor(mergedT[:, bass.ds(i * 2 + s, 1), :], t1[:, s:s + 1, :],
                                            t2[:, s:s + 1, :], ALU.add).then_inc(S["dve_chain"], 1)
                    e.eng.wait_ge(S["dve_chain"], e.c["dve_chain"].next())
            e.tick()

        def residual_pe(e, src):
            for m in range(0, DC, 2):
                e.eng.wait_ge(S[e.landing()], e.landed())
                w = e.slot(ring)
                for half in range(2):
                    e.eng.wait_ge(S["tile_free"], e.c["tile"].at(-1))
                    e.dense(e.bank(), blocks(w, 8 * half, 8), [src[:, k, :] for k in range(DC)])

        def residual_dve(e):
            for m in range(DC):
                e.eng.wait_ge(S["tile_done"], e.c["tile"].next())
                nc.vector.tensor_tensor(xT[:, m, :], xT[:, m, :], e.result(), ALU.add).then_inc(S["tile_free"], 1)
                e.eng.wait_ge(S["tile_free"], e.c["tile"].at())

        a = Arena()
        row_weight = a(16, T)
        act_g = a(DC, T)
        sg, prod_g = a(2, T), a(2, T)
        lg, comb, combT = a(NB, 20), a(NB, 16), act_g[:, 0, :]
        gm, gs, pg, m1, m2, w1, w2 = (a(NB) for _ in range(7))
        d4, oh, e4, oh1, oh2, sel = (a(NB, 4) for _ in range(6))
        sel16 = a(NB, 16)

        def router_pe(e):
            e.eng.wait_ge(S[e.landing()], e.landed())
            w = e.slot(ring)
            e.eng.wait_ge(S["tile_free"], e.c["tile"].at(-1))
            o = e.bank()
            for b in range(NB):
                for k in range(DC):
                    ins = e.mm(o[:, 32 * b:32 * b + 20], blk(hT[:, k, :], b), w[:, P * k:P * k + 20], k == 0, k == DC - 1)
            ins.then_inc(S["tile_done"], 1)
            e.eng.wait_ge(S["combined"], e.c["combined"].next())
            e.eng.wait_ge(S["tile_free"], e.c["tile"].at(-1))
            o = e.bank()
            for b in range(NB):
                ins = e.eng.transpose(o[0:16, P * b:P * b + P], comb[:, b, :], ident)
            ins.then_inc(S["tile_done"], 1)
            e.eng.wait_ge(S["tile_free"], e.c["tile"].at())
            for n in range(16):
                e.eng.wait_ge(S["tile_free"], e.c["tile"].at(-1))
                e.mm(e.bank(), row(0, 16, n), combT[0:16, :]).then_inc(S["tile_done"], 1)

        def router_act(e):
            e.skip(1)
            e.eng.wait_ge(S["group_logits"], e.c["group_logits"].next())
            nc.scalar.activation(e4, d4, ACT.Exp).then_inc(S["group_exp"], 1)
            e.eng.wait_ge(S["expert_logits"], e.c["expert_logits"].next())
            nc.scalar.activation(w2, w2, ACT.Exp).then_inc(S["expert_exp"], 1)
            e.skip(17)

        def one_hot(e, dst, logits, best):
            f4 = bc1(C("first4"), NB)
            nc.vector.tensor_reduce(best, logits, AX_X, ALU.max).then_inc(S["dve_chain"], 1)
            e.eng.wait_ge(S["dve_chain"], e.c["dve_chain"].next())
            nc.vector.tensor_tensor(dst, logits, bc(best, 4), ALU.is_equal).then_inc(S["dve_chain"], 1)
            e.eng.wait_ge(S["dve_chain"], e.c["dve_chain"].next())
            nc.vector.tensor_tensor(dst, dst, f4, ALU.mult).then_inc(S["dve_chain"], 1)
            e.eng.wait_ge(S["dve_chain"], e.c["dve_chain"].next())
            nc.vector.tensor_reduce(gs, dst, AX_X, ALU.max).then_inc(S["dve_chain"], 1)
            e.eng.wait_ge(S["dve_chain"], e.c["dve_chain"].next())
            nc.vector.tensor_tensor(dst, dst, bc(gs, 4), ALU.is_equal).then_inc(S["dve_chain"], 1)
            e.eng.wait_ge(S["dve_chain"], e.c["dve_chain"].next())

        def router_dve(e):
            e.eng.wait_ge(S["tile_done"], e.c["tile"].next())
            t = e.result()[:, 0:P].rearrange("p (b n) -> p b n", b=NB)[:, :, 0:20]
            nc.vector.tensor_tensor(lg, t, bc1(V("b_router"), NB), ALU.add).then_inc(S["tile_free"], 1)
            e.eng.wait_ge(S["tile_free"], e.c["tile"].at())
            one_hot(e, oh, lg[:, :, 0:4], gm)
            nc.vector.tensor_tensor(d4, lg[:, :, 0:4], bc(gm, 4), ALU.subtract).then_inc(S["group_logits"], 1)
            e.eng.wait_ge(S["group_exp"], e.c["group_exp"].next())
            nc.vector.tensor_reduce(gs, e4, AX_X, ALU.add).then_inc(S["dve_chain"], 1)
            e.eng.wait_ge(S["dve_chain"], e.c["dve_chain"].next())
            nc.vector.reciprocal(pg, gs).then_inc(S["dve_chain"], 1)
            e.eng.wait_ge(S["dve_chain"], e.c["dve_chain"].next())
            for g in range(4):
                nc.vector.tensor_tensor(sel16[:, :, 4 * g:4 * g + 4], lg[:, :, 4 + 4 * g:8 + 4 * g],
                                        oh[:, :, g:g + 1].to_broadcast([P, NB, 4]), ALU.mult).then_inc(S["dve_chain"], 1)
                e.eng.wait_ge(S["dve_chain"], e.c["dve_chain"].next())
            nc.vector.tensor_reduce(sel, sel16.rearrange("p b (g e) -> p b e g", g=4), AX_X, ALU.add)\
                .then_inc(S["dve_chain"], 1)
            e.eng.wait_ge(S["dve_chain"], e.c["dve_chain"].next())
            one_hot(e, oh1, sel, m1)
            nc.vector.scalar_tensor_tensor(out=sel, in0=oh1, scalar=-3.0e38, in1=sel, op0=ALU.mult, op1=ALU.add)\
                .then_inc(S["dve_chain"], 1)
            e.eng.wait_ge(S["dve_chain"], e.c["dve_chain"].next())
            one_hot(e, oh2, sel, m2)
            nc.vector.tensor_tensor(w2, m2, m1, ALU.subtract).then_inc(S["expert_logits"], 1)
            e.eng.wait_ge(S["expert_exp"], e.c["expert_exp"].next())
            nc.vector.tensor_scalar(w1, w2, 1.0, None, ALU.add).then_inc(S["dve_chain"], 1)
            e.eng.wait_ge(S["dve_chain"], e.c["dve_chain"].next())
            nc.vector.reciprocal(w1, w1).then_inc(S["dve_chain"], 1)
            e.eng.wait_ge(S["dve_chain"], e.c["dve_chain"].next())
            nc.vector.tensor_tensor(w1, w1, pg, ALU.mult).then_inc(S["dve_chain"], 1)
            e.eng.wait_ge(S["dve_chain"], e.c["dve_chain"].next())
            nc.vector.tensor_tensor(w2, w2, w1, ALU.mult).then_inc(S["dve_chain"], 1)
            e.eng.wait_ge(S["dve_chain"], e.c["dve_chain"].next())
            nc.vector.tensor_tensor(oh1, oh1, bc(w1, 4), ALU.mult).then_inc(S["dve_chain"], 1)
            e.eng.wait_ge(S["dve_chain"], e.c["dve_chain"].next())
            nc.vector.tensor_tensor(oh2, oh2, bc(w2, 4), ALU.mult).then_inc(S["dve_chain"], 1)
            e.eng.wait_ge(S["dve_chain"], e.c["dve_chain"].next())
            nc.vector.tensor_tensor(oh1, oh1, oh2, ALU.add).then_inc(S["dve_chain"], 1)
            e.eng.wait_ge(S["dve_chain"], e.c["dve_chain"].next())
            for g in range(4):
                ins = nc.vector.tensor_tensor(comb[:, :, 4 * g:4 * g + 4], oh1,
                                              oh[:, :, g:g + 1].to_broadcast([P, NB, 4]), ALU.mult)
            ins.then_inc(S["combined"], 1)
            e.eng.wait_ge(S["tile_done"], e.c["tile"].next())
            nc.vector.tensor_copy(combT[0:16, :], e.result()[0:16, :]).then_inc(S["tile_free"], 1)
            e.eng.wait_ge(S["tile_free"], e.c["tile"].at())
            for n in range(16):
                e.eng.wait_ge(S["tile_done"], e.c["tile"].next())
                nc.vector.tensor_copy(row_weight[:, n, :], e.result()).then_inc(S["tile_free"], 1)
                e.eng.wait_ge(S["tile_free"], e.c["tile"].at())
            e.tick()

        def experts_pe(e):
            with loop(e, 4, fill=12, tile=24, acts=1):
                for n in range(8):
                    e.eng.wait_ge(S[e.landing()], e.landed())
                    w = e.slot(ring)
                    for half in range(2):
                        e.eng.wait_ge(S["tile_free"], e.c["tile"].at(-1))
                        e.dense(e.bank(), blocks(w, 8 * half, 8), [hT[:, k, :] for k in range(DC)])
                e.eng.wait_ge(S["acts"], e.c["acts"].next())
                residual_pe(e, act_g)

        def experts_act(e):
            with loop(e, 4, tile=24):
                for n in range(8):
                    e.eng.wait_ge(S["tile_done"], e.c["tile"].next())
                    t = e.result()
                    e.eng.wait_ge(S["tile_free"], e.c["tile"].at(-1))
                    nc.scalar.activation(sg[:, n % 2, :], t, ACT.Silu).then_inc(S["tile_free"], 1)
                    e.eng.wait_ge(S["tile_free"], e.c["tile"].at())
                    e.skip(1)
                e.skip(8)

        def experts_dve(e):
            with loop(e, 4, tile=24, dve_chain=7) as g:
                for n in range(8):
                    e.eng.wait_ge(S["tile_free"], e.c["tile"].next())
                    e.eng.wait_ge(S["tile_done"], e.c["tile"].next())
                    nc.vector.tensor_tensor(prod_g[:, n % 2, :], e.result(), sg[:, n % 2, :], ALU.mult)\
                        .then_inc(S["tile_free"], 1)
                    e.eng.wait_ge(S["tile_free"], e.c["tile"].at())
                    ins = nc.vector.tensor_tensor(act_g[:, n, :], prod_g[:, n % 2, :], dyn(row_weight, g * 4 + n // 2), ALU.mult)
                    if n < 7:
                        ins.then_inc(S["dve_chain"], 1)
                        e.eng.wait_ge(S["dve_chain"], e.c["dve_chain"].next())
                ins.then_inc(S["acts"], 1)
                residual_dve(e)
            e.tick()

        a = Arena()
        p_tok, pT = a(NB, 256), a(2, T)
        pg_s, pt_ = a(2, T), a(2, T)

        def ple_pe(e):
            e.eng.wait_ge(S["p_in"], 16)
            for c in range(2):
                e.eng.wait_ge(S["tile_free"], e.c["tile"].at(-1))
                o = e.bank()
                for b in range(NB):
                    ins = e.eng.transpose(blk(o, b), p_tok[:, b, P * c:P * c + P], ident)
                ins.then_inc(S["tile_done"], 1)
            e.eng.wait_ge(S["tile_free"], e.c["tile"].at())
            with loop(e, 2, fill=4, tile=8):
                for s in range(4):
                    e.eng.wait_ge(S[e.landing()], e.landed())
                    w = e.slot(ring)
                    e.eng.wait_ge(S["tile_free"], e.c["tile"].at(-1))
                    e.dense(e.bank(), blocks(w, 0, 8), [hT[:, k, :] for k in range(DC)])
                    e.eng.wait_ge(S["tile_free"], e.c["tile"].at(-1))
                    e.dense(e.bank(), blocks(w, 8, 2), [pT[:, k, :] for k in range(2)])

        def ple_act(e):
            nc.scalar.dma_start(p_tok, p.rearrange("l o (b p) d -> p (l o b) d", p=P)).then_inc(S["p_in"], 16)
            e.skip(2)
            with loop(e, 2, tile=8):
                for s in range(4):
                    e.eng.wait_ge(S["tile_done"], e.c["tile"].next())
                    t = e.result()
                    e.eng.wait_ge(S["tile_free"], e.c["tile"].at(-1))
                    nc.scalar.activation(pg_s[:, s % 2, :], t, ACT.Sigmoid).then_inc(S["tile_free"], 1)
                    e.eng.wait_ge(S["tile_free"], e.c["tile"].at())
                    e.skip(1)

        def ple_dve(e):
            for c in range(2):
                e.eng.wait_ge(S["tile_done"], e.c["tile"].next())
                nc.vector.tensor_copy(pT[:, c, :], e.result()).then_inc(S["tile_free"], 1)
                e.eng.wait_ge(S["tile_free"], e.c["tile"].at())
            with loop(e, 2, tile=8, dve_chain=4) as i:
                for s in range(4):
                    e.eng.wait_ge(S["tile_free"], e.c["tile"].next())
                    e.eng.wait_ge(S["tile_done"], e.c["tile"].next())
                    nc.vector.tensor_tensor(pt_[:, s % 2, :], e.result(), pg_s[:, s % 2, :], ALU.mult)\
                        .then_inc(S["tile_free"], 1)
                    e.eng.wait_ge(S["tile_free"], e.c["tile"].at())
                    xm = dyn(xT, i * 4 + s)
                    nc.vector.tensor_tensor(xm, xm, pt_[:, s % 2, :], ALU.add).then_inc(S["dve_chain"], 1)
                    e.eng.wait_ge(S["dve_chain"], e.c["dve_chain"].next())
            e.tick()

        a = Arena()
        kr = a(T)
        cq, ckv = a(2, T), a(1, T)
        v_tok, o_tok2 = a(NB, T), a(NB, T)
        mla_at = a.at
        upad, ys, gsig = a(4, 30 + T), a(4, T), a(2, T)
        PE_TAPS = 15
        diag = a(4, PE_TAPS, P)
        a = Arena(mla_at)
        LS = Soft(a)
        qs, ks, rtmp = a(2, T), a(2, T), a(2, T)
        qh = hT
        assert a.at <= WORK - 1024
        mla_mask = Arena(a.at)(T)
        catT = mixT
        kh = ring_like = Arena(a.at + T)(MH, T) if a.at + T + MH * T <= WORK else None

        def glu_pe(e):
            for j in range(4):
                e.eng.wait_ge(S[e.landing()], e.landed())
                w = e.slot(ring)
                for half in range(2):
                    e.eng.wait_ge(S["tile_free"], e.c["tile"].at(-1))
                    e.dense(e.bank(), blocks(w, 8 * half, 8), [hT[:, k, :] for k in range(DC)])
            for n in range(2):
                e.eng.wait_ge(S[e.landing()], e.landed())
                w = e.slot(ring)
                for half in range(2):
                    rows_ = 96 if n and half else P
                    e.eng.wait_ge(S["tile_free"], e.c["tile"].at(-1))
                    e.dense(e.bank()[0:rows_, :], blocks(w, 8 * half, 8, rows_), [hT[:, k, :] for k in range(DC)])
            e.eng.wait_ge(S["upad"], e.c["upad"].next())
            for j in range(4):
                e.eng.wait_ge(S["diagonals"], e.c["diagonals"].next())
                for t in range(PE_TAPS):
                    ins = e.mm(bank[:, j, :], diag[:, j, t, :], upad[:, j, t:t + T], t == 0, t == PE_TAPS - 1)
                ins.then_inc(S["filter_part"], 1)
            for rnd in range(2):
                e.eng.wait_ge(S["tile_free"], e.c["tile"].at(-1))
                o = e.bank()
                for k in range(4):
                    if rnd == 1:
                        e.eng.wait_ge(S["squares"], e.c["squares"].next())
                    elif k == 0:
                        e.eng.wait_ge(S["channels"], e.c["channels"].next())
                    ins = e.mm(o, ones, (ys if rnd == 0 else squares)[:, k, :], k == 0, k == 3)
                ins.then_inc(S["tile_done"], 1)

        def glu_act(e):
            cw = V("conv0_w").rearrange("p (j t) -> p j t", t=31)
            for j in range(4):
                for t in range(PE_TAPS):
                    ins = nc.scalar.activation(diag[:, j, t, :], ident, ACT.Copy, scale=cw[:, j, t:t + 1])
                ins.then_inc(S["diagonals"], 1)
            for j in range(4):
                e.eng.wait_ge(S["tile_free"], e.c["tile"].next())
                e.eng.wait_ge(S["tile_done"], e.c["tile"].next())
                t = e.result()
                e.eng.wait_ge(S["tile_free"], e.c["tile"].at(-1))
                nc.scalar.activation(gsig[:, j % 2, :], t, ACT.Sigmoid).then_inc(S["tile_free"], 1)
                e.eng.wait_ge(S["tile_free"], e.c["tile"].at())
            e.skip(4)
            e.eng.wait_ge(S["tile_free"], e.c["tile"].next())
            for k in range(4):
                e.eng.wait_ge(S["centred"], e.c["centred"].next())
                nc.scalar.activation(squares[:, k, :], ys[:, k, :], ACT.Square).then_inc(S["squares"], 1)
            e.eng.wait_ge(S["tile_free"], e.c["tile"].next())
            nc.scalar.activation(spread, spread, ACT.Sqrt).then_inc(S["root"], 1)
            for k in range(4):
                e.eng.wait_ge(S["ln_out"], e.c["ln_out"].next())
                nc.scalar.activation(catT[:, k, :], ys[:, k, :], ACT.Silu, bias=V("ln_b")[:, k:k + 1])\
                    .then_inc(S["ln_silu"], 1)

        def glu_dve(e):
            nc.vector.memset(upad[:, :, 0:30], 0.0).then_inc(S["dve_chain"], 1)
            e.eng.wait_ge(S["dve_chain"], e.c["dve_chain"].next())
            for j in range(4):
                u = upad[:, j, 30:30 + T]
                e.eng.wait_ge(S["tile_done"], e.c["tile"].next())
                nc.vector.tensor_copy(u, e.result()).then_inc(S["tile_free"], 1)
                e.eng.wait_ge(S["tile_free"], e.c["tile"].at())
                e.eng.wait_ge(S["tile_free"], e.c["tile"].next())
                nc.vector.tensor_tensor(u, u, gsig[:, j % 2, :], ALU.mult).then_inc(S["dve_chain"], 1)
                e.eng.wait_ge(S["dve_chain"], e.c["dve_chain"].next())
            nc.vector.memset(e.ticks, 0.0).then_inc(S["upad"], 1)
            for dst in (cq[:, 0, :], cq[:, 1, :], ckv[:, 0, :]):
                e.eng.wait_ge(S["tile_done"], e.c["tile"].next())
                nc.vector.tensor_copy(dst, e.result()).then_inc(S["tile_free"], 1)
                e.eng.wait_ge(S["tile_free"], e.c["tile"].at())
            e.eng.wait_ge(S["tile_done"], e.c["tile"].next())
            nc.vector.tensor_copy(kr[0:96, :], e.result()[0:96, :]).then_inc(S["tile_free"], 1)
            e.eng.wait_ge(S["tile_free"], e.c["tile"].at())
            cw = V("conv0_w").rearrange("p (j t) -> p j t", t=31)
            first = PE_TAPS
            for j in range(4):
                nc.vector.tensor_scalar(ys[:, j, :], upad[:, j, first:first + T], cw[:, j, first:first + 1],
                                        V("conv0_b")[:, j:j + 1], ALU.mult, ALU.add).then_inc(S["dve_chain"], 1)
                e.eng.wait_ge(S["dve_chain"], e.c["dve_chain"].next())
            with loop(e, 30 - first, dve_chain=4) as tap:
                for j in range(4):
                    nc.vector.scalar_tensor_tensor(
                 out=ys[:, j, :], in0=upad[:, j, bass.ds(tap + (first + 1), T)],
                 scalar=cw[:, j, bass.ds(tap + (first + 1), 1)],
                 in1=ys[:, j, :], op0=ALU.mult, op1=ALU.add).then_inc(S["dve_chain"], 1)
                    e.eng.wait_ge(S["dve_chain"], e.c["dve_chain"].next())
            for j in range(4):
                e.eng.wait_ge(S["filter_part"], e.c["filter_part"].next())
                nc.vector.tensor_tensor(ys[:, j, :], ys[:, j, :], bank[:, j, :], ALU.add).then_inc(S["dve_chain"], 1)
                e.eng.wait_ge(S["dve_chain"], e.c["dve_chain"].next())
            nc.vector.memset(e.ticks, 0.0).then_inc(S["channels"], 1)
            e.eng.wait_ge(S["tile_done"], e.c["tile"].next())
            nc.vector.tensor_scalar(rstd, e.result(), 1.0 / 512, None, ALU.mult).then_inc(S["tile_free"], 1)
            e.eng.wait_ge(S["tile_free"], e.c["tile"].at())
            for j in range(4):
                nc.vector.tensor_tensor(ys[:, j, :], ys[:, j, :], rstd, ALU.subtract).then_inc(S["centred"], 1)
            e.eng.wait_ge(S["tile_done"], e.c["tile"].next())
            nc.vector.tensor_scalar(spread, e.result(), 1.0 / 512, LN_EPS, ALU.mult, ALU.add).then_inc(S["tile_free"], 1)
            e.eng.wait_ge(S["tile_free"], e.c["tile"].at())
            e.eng.wait_ge(S["root"], e.c["root"].next())
            nc.vector.reciprocal(rstd, spread).then_inc(S["dve_chain"], 1)
            e.eng.wait_ge(S["dve_chain"], e.c["dve_chain"].next())
            for j in range(4):
                nc.vector.scalar_tensor_tensor(out=ys[:, j, :], in0=ys[:, j, :], scalar=V("ln_g")[:, j:j + 1], in1=rstd,
                                               op0=ALU.mult, op1=ALU.mult).then_inc(S["ln_out"], 1)
            for j in range(4):
                e.eng.wait_ge(S["ln_silu"], e.c["ln_silu"].next())
            e.tick()

        rot = C("rope_rot", 96)

        def latent_pe(e):
            e.eng.wait_ge(S[e.landing()], e.landed())
            w = e.slot(ring)
            for h in range(MH):
                e.eng.wait_ge(S["tile_free"], e.c["tile"].at(-1))
                e.dense(e.bank()[0:96, :], blocks(w, 2 * h, 2, 96), [cq[:, k, :] for k in range(2)])
            e.eng.wait_ge(S["tile_free"], e.c["tile"].at())
            for h in range(MH):
                e.eng.wait_ge(S["tile_free"], e.c["tile"].at(-1))
                e.mm(e.bank()[0:96, :], rot, qh[0:96, h, :]).then_inc(S["tile_done"], 1)
            e.eng.wait_ge(S["tile_free"], e.c["tile"].at(-1))
            e.mm(e.bank()[0:96, :], rot, kr[0:96, :]).then_inc(S["tile_done"], 1)
            e.eng.wait_ge(S[e.landing()], e.landed())
            w = e.slot(ring)
            for h in range(MH):
                e.eng.wait_ge(S["tile_free"], e.c["tile"].at(-1))
                o = e.bank()
                e.mm(o[0:64, 0:256], w[:, P * h:P * h + 64], ckv[:, 0, 0:256])
                e.mm(o[0:64, 256:512], w[:, P * h:P * h + 64], ckv[:, 0, 256:512]).then_inc(S["tile_done"], 1)
            for b in range(NB):
                e.eng.wait_ge(S["tile_free"], e.c["tile"].at(-1))
                e.mm(e.bank(), blk(ckv[:, 0, :], b), w[:, 1024:1536]).then_inc(S["tile_done"], 1)

        def latent_dve(e):
            cos, sin = C("rope_cos", 96), C("rope_sin", 96)
            for h in range(MH):
                e.eng.wait_ge(S["tile_done"], e.c["tile"].next())
                nc.vector.tensor_copy(qh[0:96, h, :], e.result()[0:96, :]).then_inc(S["tile_free"], 1)
                e.eng.wait_ge(S["tile_free"], e.c["tile"].at())
            for h in range(MH + 1):
                src = qh[0:96, h, :] if h < MH else kr[0:96, :]
                r = rtmp[0:96, h % 2, :]
                e.eng.wait_ge(S["tile_done"], e.c["tile"].next())
                nc.vector.tensor_tensor(r, e.result()[0:96, :], sin, ALU.mult).then_inc(S["tile_free"], 1)
                e.eng.wait_ge(S["tile_free"], e.c["tile"].at())
                nc.vector.tensor_tensor(src, src, cos, ALU.mult).then_inc(S["dve_chain"], 1)
                e.eng.wait_ge(S["dve_chain"], e.c["dve_chain"].next())
                nc.vector.tensor_tensor(src, src, r, ALU.add).then_inc(S["dve_chain"], 1)
                e.eng.wait_ge(S["dve_chain"], e.c["dve_chain"].next())
            for h in range(MH):
                e.eng.wait_ge(S["tile_done"], e.c["tile"].next())
                nc.vector.tensor_copy(kh[0:64, h, :], e.result()[0:64, :]).then_inc(S["tile_free"], 1)
                e.eng.wait_ge(S["tile_free"], e.c["tile"].at())
                nc.vector.tensor_copy(kh[64:96, h, :], kr[64:96, :])
            for b in range(NB):
                e.eng.wait_ge(S["tile_done"], e.c["tile"].next())
                nc.vector.tensor_copy(v_tok[:, b, :], e.result()).then_inc(S["tile_free"], 1)
                e.eng.wait_ge(S["tile_free"], e.c["tile"].at())
            nc.vector.memset(mla_mask[:, 0:384], 0.0).then_inc(S["dve_chain"], 1)
            e.eng.wait_ge(S["dve_chain"], e.c["dve_chain"].next())
            nc.vector.tensor_copy(mla_mask[:, 384:512], C("mla_mask")).then_inc(S["dve_chain"], 1)
            e.eng.wait_ge(S["dve_chain"], e.c["dve_chain"].next())
            e.tick()

        widths = [P * (b + 1) for b in range(NB)]

        def mla_pe(e):
            with loop(e, MH // 2, head_q=1, head_k=1, probs=8, turned_a=8, turned_b=8, unit_out=8) as pair:
                e.eng.wait_ge(S["head_q"], e.c["head_q"].next())
                e.eng.wait_ge(S["head_k"], e.c["head_k"].next())
                units = []
                for s in range(2):
                    for b in range(NB):
                        vals = [v_tok[:, k, bass.ds(pair * (2 * VD) + s * VD, VD)] for k in range(b + 1)]
                        units.append((widths[b], [(0, widths[b], blk(qs[0:96, s, :], b), ks[0:96, s, 0:widths[b]])], vals))
                unit_pe(e, LS, units)
            tokens_to_features_pe(e, o_tok2, False)

        def mla_act(e):
            with loop(e, MH // 2, maxima=8, turned=8, heads=1) as pair:
                e.eng.wait_ge(S["heads"], e.c["heads"].next())
                nc.scalar.activation(ks[0:96, :, :], kh[0:96, bass.ds(pair * 2, 2), :], ACT.Copy)\
                    .then_inc(S["head_k"], 1)
                unit_act(e, LS, widths * 2)
            e.skip(4)

        def mla_dve(e):
            with loop(e, MH // 2, scores=8, turned=8, mixed=8, dve_chain=16) as pair:
                nc.vector.tensor_copy(qs[0:96, :, :], qh[0:96, bass.ds(pair * 2, 2), :]).then_inc(S["head_q"], 1)
                nc.vector.memset(e.ticks, 0.0).then_inc(S["heads"], 1)
                outs = [o_tok2[:, b, bass.ds(pair * (2 * VD) + s * VD, VD)] for s in range(2) for b in range(NB)]
                unit_dve(e, LS, widths * 2, [mla_mask[:, 512 - w:512] for w in widths] * 2, (NOPE + ROPE) ** -0.5, outs)
            tokens_to_features_dve(e, catT[:, 4:8, :], False)
            e.tick()

        a = Arena()
        ff = a(FC, T)
        fpad, fy = a(2, 2 + T), a(2, T)
        fgate = a(T)
        fw, fb = a(2, 3), a(2, 1)
        FF_TAIL = FC % 4

        def ffn_pe(e):
            def up():
                e.eng.wait_ge(S[e.landing()], e.landed())
                w = e.slot(ring)
                for half in range(2):
                    e.eng.wait_ge(S["tile_free"], e.c["tile"].at(-1))
                    e.dense(e.bank(), blocks(w, 8 * half, 8), [hT[:, k, :] for k in range(DC)])
            with loop(e, FC // 4, fill=4, tile=8):
                for s in range(4):
                    up()
            for s in range(FF_TAIL):
                up()
            e.eng.wait_ge(S["ff_ready"], e.c["ff_ready"].next())
            with loop(e, DC // 2, fill=4, tile=2):
                for s in range(2):
                    e.eng.wait_ge(S["tile_free"], e.c["tile"].at(-1))
                    o = e.bank()
                    for part in range(2):
                        e.eng.wait_ge(S[e.landing()], e.landed())
                        w = e.slot(ring)
                        for k in range(FC // 2):
                            kk = part * (FC // 2) + k
                            ins = e.mm(o, w[:, P * k:P * k + P], ff[:, kk, :], kk == 0, kk == FC - 1)
                    ins.then_inc(S["tile_done"], 1)

        def ffn_act(e):
            def up():
                e.eng.wait_ge(S["pads_free"], e.c["pads_free"].next())
                for half in range(2):
                    e.eng.wait_ge(S["tile_done"], e.c["tile"].next())
                    t = e.result()
                    e.eng.wait_ge(S["tile_free"], e.c["tile"].at(-1))
                    nc.scalar.activation(fpad[:, half, 2:2 + T], t, ACT.Copy).then_inc(S["tile_free"], 1)
                    e.eng.wait_ge(S["tile_free"], e.c["tile"].at())
                e.eng.wait_ge(S["gate_ready"], e.c["gate_ready"].next())
                nc.scalar.activation(fgate, fy[:, 0, :], ACT.Silu).then_inc(S["gate_silu"], 1)
            with loop(e, FC // 4, tile=8, pads_free=4, gate_ready=4):
                for s in range(4):
                    up()
            for s in range(FF_TAIL):
                up()
            e.skip(DC)

        def ffn_dve(e, wname, bname):
            fwv = V(wname).rearrange("p (j n) -> p j n", n=6)
            fbv = V(bname).rearrange("p (j n) -> p j n", n=2)
            nc.vector.memset(fpad[:, :, 0:2], 0.0).then_inc(S["dve_chain"], 1)
            e.eng.wait_ge(S["dve_chain"], e.c["dve_chain"].next())

            def up(j):
                nc.vector.tensor_copy(fw.rearrange("p a b -> p (a b)"), dyn(fwv, j)).then_inc(S["dve_chain"], 1)
                e.eng.wait_ge(S["dve_chain"], e.c["dve_chain"].next())
                nc.vector.tensor_copy(fb.rearrange("p a b -> p (a b)"), dyn(fbv, j)).then_inc(S["pads_free"], 1)
                e.eng.wait_ge(S["pads_free"], e.c["pads_free"].next())
                for half in range(2):
                    e.eng.wait_ge(S["tile_free"], e.c["tile"].next())
                    y = fy[:, half, :]
                    nc.vector.tensor_scalar(y, fpad[:, half, 2:2 + T], fw[:, half, 2:3], fb[:, half, :],
                                            ALU.mult, ALU.add).then_inc(S["dve_chain"], 1)
                    e.eng.wait_ge(S["dve_chain"], e.c["dve_chain"].next())
                    for t in range(2):
                        ins = nc.vector.scalar_tensor_tensor(out=y, in0=fpad[:, half, t:t + T], scalar=fw[:, half, t:t + 1],
                                                             in1=y, op0=ALU.mult, op1=ALU.add)
                        if (half, t) != (0, 1):
                            ins.then_inc(S["dve_chain"], 1)
                            e.eng.wait_ge(S["dve_chain"], e.c["dve_chain"].next())
                    if half == 0:
                        ins.then_inc(S["gate_ready"], 1)
                e.eng.wait_ge(S["gate_silu"], e.c["gate_silu"].next())
                nc.vector.tensor_tensor(dyn(ff, j), fgate, fy[:, 1, :], ALU.mult).then_inc(S["dve_chain"], 1)
                e.eng.wait_ge(S["dve_chain"], e.c["dve_chain"].next())

            with loop(e, FC // 4, tile=8, pads_free=4, gate_silu=4, dve_chain=28) as i:
                for s in range(4):
                    up(i * 4 + s)
            for s in range(FF_TAIL):
                up(FC - FF_TAIL + s)
            nc.vector.memset(e.ticks, 0.0).then_inc(S["ff_ready"], 1)
            with loop(e, DC // 2, tile=2) as i:
                for s in range(2):
                    xm = dyn(xT, i * 2 + s)
                    e.eng.wait_ge(S["tile_done"], e.c["tile"].next())
                    nc.vector.tensor_tensor(xm, xm, e.result(), ALU.add).then_inc(S["tile_free"], 1)
                    e.eng.wait_ge(S["tile_free"], e.c["tile"].at())
            e.tick()

        Q, NP_ = 4, 16
        a = Arena()
        uT = a(4, T)
        ushift = a(NP_, P)
        c_re, c_im = a(NP_, 8, 32), a(NP_, 8, 32)
        bT_re, bT_im = a(NP_, P), a(NP_, P)
        toep = a(NP_, P)
        small = a(24, NP_)
        ints = a(2, NP_)
        ssm_in = a(4, NP_, NP_)
        tmp1, tmp2 = a(NP_, NP_), a(NP_, NP_)
        b_re = mixT[:, 0:4, :].rearrange("p a n -> p (a n)").rearrange("p (a b c) -> p a b c", a=NP_, b=Q)
        b_im = mixT[:, 4:8, :].rearrange("p a n -> p (a n)").rearrange("p (a b c) -> p a b c", a=NP_, b=Q)
        bb_re = mixT[:, 8, 0:256].rearrange("p (a b) -> p a b", a=NP_)
        bb_im = mixT[:, 8, 256:512].rearrange("p (a b) -> p a b", a=NP_)

        def quarters(n, src):
            return src[:, 4 * n:4 * n + 4, :].rearrange("p a n -> p (a n)").rearrange("p (a b) -> p a b", a=NP_)

        turn_re, turn_im = quarters(0, hT), quarters(1, hT)
        v_re, v_im, decay4 = quarters(0, mixT), quarters(1, mixT), quarters(2, mixT)
        z_re, z_im = bT_re, bT_im
        xs_re, xs_im = None, None
        (dt_, th, mag, kf, thr, half_s, sn, cs, sx, lre, lim, nre, den, fre, fim, pre, pim, q1, q2, rho, wre, wim,
         q3, q4) = (small[:, n, :] for n in range(24))
        C_HI, C_LO = 6.28125, 2 * np.pi - 6.28125

        def cmul(e, o_re, o_im, ar, ai, br, bi, t_1, t_2):
            nc.vector.tensor_tensor(t_1, ar, br, ALU.mult).then_inc(S["dve_chain"], 1)
            e.eng.wait_ge(S["dve_chain"], e.c["dve_chain"].next())
            nc.vector.tensor_tensor(t_2, ai, bi, ALU.mult).then_inc(S["dve_chain"], 1)
            e.eng.wait_ge(S["dve_chain"], e.c["dve_chain"].next())
            nc.vector.tensor_tensor(o_re, t_1, t_2, ALU.subtract).then_inc(S["dve_chain"], 1)
            e.eng.wait_ge(S["dve_chain"], e.c["dve_chain"].next())
            nc.vector.tensor_tensor(t_1, ar, bi, ALU.mult).then_inc(S["dve_chain"], 1)
            e.eng.wait_ge(S["dve_chain"], e.c["dve_chain"].next())
            nc.vector.tensor_tensor(t_2, ai, br, ALU.mult).then_inc(S["dve_chain"], 1)
            e.eng.wait_ge(S["dve_chain"], e.c["dve_chain"].next())
            nc.vector.tensor_tensor(o_im, t_1, t_2, ALU.add).then_inc(S["dve_chain"], 1)
            e.eng.wait_ge(S["dve_chain"], e.c["dve_chain"].next())

        def ssm_setup_pe(e):
            for m in range(0, 4, 2):
                e.eng.wait_ge(S[e.landing()], e.landed())
                w = e.slot(ring)
                for half in range(2):
                    e.eng.wait_ge(S["tile_free"], e.c["tile"].at(-1))
                    e.dense(e.bank(), blocks(w, 8 * half, 8), [hT[:, k, :] for k in range(DC)])
            e.eng.wait_ge(S["b_ready"], e.c["b_ready"].next())
            for src in (b_re, b_im):
                for n in range(0, NP_, 4):
                    e.eng.wait_ge(S["tile_free"], e.c["tile"].at(-1))
                    o = e.bank()
                    for j in range(4):
                        ins = e.eng.transpose(blk(o, j), src[:, n + j, :, :].rearrange("p t c -> p (t c)"), ident)
                    ins.then_inc(S["tile_done"], 1)
            for n in range(0, NP_, 4):
                e.eng.wait_ge(S["tile_free"], e.c["tile"].at(-1))
                o = e.bank()
                for j in range(4):
                    for t in range(Q):
                        lags = slice(3 - t, 7 - t)
                        oo = blk(o, j)[32 * t:32 * t + 32, :]
                        cr = c_re[:, n + j, lags, :].rearrange("p l c -> p (l c)")
                        ci = c_im[:, n + j, lags, :].rearrange("p l c -> p (l c)")
                        e.mm(oo, b_re[:, n + j, 3, :], cr, True, False)
                        ins = e.mm(oo, b_im[:, n + j, 3, :], ci, False, True)
                ins.then_inc(S["tile_done"], 1)

        def ssm_setup_act(e):
            nc.scalar.dma_start(ssm_in, ssm).then_inc(S["ssm_in"], 16)
            nc.scalar.activation(dt_, V("s_dt"), ACT.Exp).then_inc(S["dt"], 1)
            e.eng.wait_ge(S["decay_exponent"], e.c["decay_exponent"].next())
            nc.scalar.activation(mag, mag, ACT.Exp).then_inc(S["mag"], 1)
            e.eng.wait_ge(S["angle"], e.c["angle"].next())
            nc.scalar.activation(sn, thr, ACT.Sin)
            nc.scalar.activation(half_s, q3, ACT.Sin).then_inc(S["sines"], 1)
            e.skip(4 + 8 + 4)

        def ssm_setup_dve(e):
            for j in range(4):
                e.eng.wait_ge(S["tile_done"], e.c["tile"].next())
                nc.vector.tensor_copy(uT[:, j, :], e.result()).then_inc(S["tile_free"], 1)
                e.eng.wait_ge(S["tile_free"], e.c["tile"].at())
            for q in range(4):
                for t in range(Q):
                    nc.vector.tensor_copy(ushift[32 * t:32 * t + 32, :, :].rearrange("p (j q) m -> p q j m", q=4)[:, q],
                                          uT[32 * q:32 * q + 32, :, t::4])
            e.eng.wait_ge(S["dt"], e.c["dt"].next())
            nc.vector.tensor_tensor(mag, V("s_are"), dt_, ALU.mult).then_inc(S["decay_exponent"], 1)
            nc.vector.tensor_tensor(th, V("s_aim"), dt_, ALU.mult).then_inc(S["dve_chain"], 1)
            e.eng.wait_ge(S["dve_chain"], e.c["dve_chain"].next())
            nc.vector.tensor_scalar(kf, th, 1.0 / (2 * np.pi), None, ALU.mult).then_inc(S["dve_chain"], 1)
            e.eng.wait_ge(S["dve_chain"], e.c["dve_chain"].next())
            nc.vector.tensor_copy(ints[:, 0, :].bitcast(I32), kf).then_inc(S["dve_chain"], 1)
            e.eng.wait_ge(S["dve_chain"], e.c["dve_chain"].next())
            nc.vector.tensor_copy(kf, ints[:, 0, :].bitcast(I32)).then_inc(S["dve_chain"], 1)
            e.eng.wait_ge(S["dve_chain"], e.c["dve_chain"].next())
            nc.vector.scalar_tensor_tensor(out=thr, in0=kf, scalar=-C_HI, in1=th, op0=ALU.mult, op1=ALU.add)\
                .then_inc(S["dve_chain"], 1)
            e.eng.wait_ge(S["dve_chain"], e.c["dve_chain"].next())
            nc.vector.scalar_tensor_tensor(out=thr, in0=kf, scalar=-C_LO, in1=thr, op0=ALU.mult, op1=ALU.add)\
                .then_inc(S["dve_chain"], 1)
            e.eng.wait_ge(S["dve_chain"], e.c["dve_chain"].next())
            for lim_, op, sgn in ((3.1415925, ALU.is_gt, -1.0), (-3.1415925, ALU.is_lt, 1.0)):
                nc.vector.tensor_scalar(q1, thr, lim_, sgn * 2 * np.pi, op, ALU.mult).then_inc(S["dve_chain"], 1)
                e.eng.wait_ge(S["dve_chain"], e.c["dve_chain"].next())
                nc.vector.tensor_tensor(thr, thr, q1, ALU.add).then_inc(S["dve_chain"], 1)
                e.eng.wait_ge(S["dve_chain"], e.c["dve_chain"].next())
            nc.vector.tensor_scalar(thr, thr, 3.1415925, -3.1415925, ALU.min, ALU.max).then_inc(S["dve_chain"], 1)
            e.eng.wait_ge(S["dve_chain"], e.c["dve_chain"].next())
            nc.vector.tensor_scalar(q3, thr, 0.5, None, ALU.mult).then_inc(S["angle"], 1)
            e.eng.wait_ge(S["mag"], e.c["mag"].next())
            e.eng.wait_ge(S["sines"], e.c["sines"].next())
            nc.vector.tensor_tensor(cs, half_s, half_s, ALU.mult).then_inc(S["dve_chain"], 1)
            e.eng.wait_ge(S["dve_chain"], e.c["dve_chain"].next())
            nc.vector.tensor_scalar(cs, cs, -2.0, 1.0, ALU.mult, ALU.add).then_inc(S["dve_chain"], 1)
            e.eng.wait_ge(S["dve_chain"], e.c["dve_chain"].next())
            nc.vector.tensor_tensor(lre, mag, cs, ALU.mult).then_inc(S["dve_chain"], 1)
            e.eng.wait_ge(S["dve_chain"], e.c["dve_chain"].next())
            nc.vector.tensor_tensor(lim, mag, sn, ALU.mult).then_inc(S["dve_chain"], 1)
            e.eng.wait_ge(S["dve_chain"], e.c["dve_chain"].next())
            ar, ai = V("s_are"), V("s_aim")
            nc.vector.tensor_scalar(nre, lre, -1.0, None, ALU.add).then_inc(S["dve_chain"], 1)
            e.eng.wait_ge(S["dve_chain"], e.c["dve_chain"].next())
            nc.vector.tensor_tensor(den, ar, ar, ALU.mult).then_inc(S["dve_chain"], 1)
            e.eng.wait_ge(S["dve_chain"], e.c["dve_chain"].next())
            nc.vector.tensor_tensor(q1, ai, ai, ALU.mult).then_inc(S["dve_chain"], 1)
            e.eng.wait_ge(S["dve_chain"], e.c["dve_chain"].next())
            nc.vector.tensor_tensor(den, den, q1, ALU.add).then_inc(S["dve_chain"], 1)
            e.eng.wait_ge(S["dve_chain"], e.c["dve_chain"].next())
            nc.vector.reciprocal(den, den).then_inc(S["dve_chain"], 1)
            e.eng.wait_ge(S["dve_chain"], e.c["dve_chain"].next())
            nc.vector.tensor_tensor(q1, nre, ar, ALU.mult).then_inc(S["dve_chain"], 1)
            e.eng.wait_ge(S["dve_chain"], e.c["dve_chain"].next())
            nc.vector.tensor_tensor(q2, lim, ai, ALU.mult).then_inc(S["dve_chain"], 1)
            e.eng.wait_ge(S["dve_chain"], e.c["dve_chain"].next())
            nc.vector.tensor_tensor(q1, q1, q2, ALU.add).then_inc(S["dve_chain"], 1)
            e.eng.wait_ge(S["dve_chain"], e.c["dve_chain"].next())
            nc.vector.tensor_tensor(fre, q1, den, ALU.mult).then_inc(S["dve_chain"], 1)
            e.eng.wait_ge(S["dve_chain"], e.c["dve_chain"].next())
            nc.vector.tensor_tensor(q1, lim, ar, ALU.mult).then_inc(S["dve_chain"], 1)
            e.eng.wait_ge(S["dve_chain"], e.c["dve_chain"].next())
            nc.vector.tensor_tensor(q2, nre, ai, ALU.mult).then_inc(S["dve_chain"], 1)
            e.eng.wait_ge(S["dve_chain"], e.c["dve_chain"].next())
            nc.vector.tensor_tensor(q1, q1, q2, ALU.subtract).then_inc(S["dve_chain"], 1)
            e.eng.wait_ge(S["dve_chain"], e.c["dve_chain"].next())
            nc.vector.tensor_tensor(fim, q1, den, ALU.mult).then_inc(S["dve_chain"], 1)
            e.eng.wait_ge(S["dve_chain"], e.c["dve_chain"].next())
            e.eng.wait_ge(S["ssm_in"], 16)
            br, bi, cr, ci = (ssm_in[:, n, :, :] for n in range(4))
            cmul(e, bb_re, bb_im, br, bi, bc(fre, 16), bc(fim, 16), tmp1, tmp2)
            for z in (b_re, b_im):
                nc.vector.memset(z, 0.0).then_inc(S["dve_chain"], 1)
                e.eng.wait_ge(S["dve_chain"], e.c["dve_chain"].next())
            for z in (c_re, c_im):
                nc.vector.memset(z, 0.0).then_inc(S["dve_chain"], 1)
                e.eng.wait_ge(S["dve_chain"], e.c["dve_chain"].next())
            nc.vector.memset(pre, 1.0).then_inc(S["dve_chain"], 1)
            e.eng.wait_ge(S["dve_chain"], e.c["dve_chain"].next())
            nc.vector.memset(pim, 0.0).then_inc(S["dve_chain"], 1)
            e.eng.wait_ge(S["dve_chain"], e.c["dve_chain"].next())
            two = ((0, 0), (64, 16))
            for lag in range(5):
                def spread_out(dst, n_, src):
                    for p0, c0 in two:
                        nc.vector.tensor_copy(dst[p0:p0 + 64, :, n_, c0:c0 + 16], src[p0:p0 + 64, :, :])\
                            .then_inc(S["dve_chain"], 1)
                        e.eng.wait_ge(S["dve_chain"], e.c["dve_chain"].next())
                if lag < 4:
                    for which in range(2):
                        x_, y_ = (bc(pre, 16), bc(pim, 16)) if which == 0 else (bc(pim, 16), bc(pre, 16))
                        nc.vector.tensor_tensor(tmp1, bb_re, x_, ALU.mult).then_inc(S["dve_chain"], 1)
                        e.eng.wait_ge(S["dve_chain"], e.c["dve_chain"].next())
                        nc.vector.tensor_tensor(tmp2, bb_im, y_, ALU.mult).then_inc(S["dve_chain"], 1)
                        e.eng.wait_ge(S["dve_chain"], e.c["dve_chain"].next())
                        nc.vector.tensor_tensor(tmp1, tmp1, tmp2, ALU.subtract if which == 0 else ALU.add)\
                            .then_inc(S["dve_chain"], 1)
                        e.eng.wait_ge(S["dve_chain"], e.c["dve_chain"].next())
                        spread_out((b_re, b_im)[which], 3 - lag, tmp1)
                nc.vector.tensor_tensor(tmp1, cr, bc(pre, 16), ALU.mult).then_inc(S["dve_chain"], 1)
                e.eng.wait_ge(S["dve_chain"], e.c["dve_chain"].next())
                nc.vector.tensor_tensor(tmp2, ci, bc(pim, 16), ALU.mult).then_inc(S["dve_chain"], 1)
                e.eng.wait_ge(S["dve_chain"], e.c["dve_chain"].next())
                nc.vector.tensor_tensor(tmp1, tmp1, tmp2, ALU.subtract).then_inc(S["dve_chain"], 1)
                e.eng.wait_ge(S["dve_chain"], e.c["dve_chain"].next())
                spread_out(c_re, 3 + lag, tmp1)
                nc.vector.tensor_tensor(tmp1, cr, bc(pim, 16), ALU.mult).then_inc(S["dve_chain"], 1)
                e.eng.wait_ge(S["dve_chain"], e.c["dve_chain"].next())
                nc.vector.tensor_tensor(tmp2, ci, bc(pre, 16), ALU.mult).then_inc(S["dve_chain"], 1)
                e.eng.wait_ge(S["dve_chain"], e.c["dve_chain"].next())
                nc.vector.scalar_tensor_tensor(out=tmp1, in0=tmp1, scalar=-1.0, in1=tmp2, op0=ALU.mult,
                                               op1=ALU.subtract).then_inc(S["dve_chain"], 1)
                e.eng.wait_ge(S["dve_chain"], e.c["dve_chain"].next())
                spread_out(c_im, 3 + lag, tmp1)
                if lag < 4:
                    cmul(e, wre, wim, pre, pim, lre, lim, q1, q2)
                    nc.vector.tensor_copy(pre, wre).then_inc(S["dve_chain"], 1)
                    e.eng.wait_ge(S["dve_chain"], e.c["dve_chain"].next())
                    nc.vector.tensor_copy(pim, wim).then_inc(S["dve_chain"], 1)
                    e.eng.wait_ge(S["dve_chain"], e.c["dve_chain"].next())
            nc.vector.memset(e.ticks, 0.0).then_inc(S["b_ready"], 1)
            e.eng.wait_ge(S["b_ready"], e.c["b_ready"].next())
            nc.vector.tensor_tensor(rho, mag, mag, ALU.mult).then_inc(S["dve_chain"], 1)
            e.eng.wait_ge(S["dve_chain"], e.c["dve_chain"].next())
            nc.vector.tensor_tensor(rho, rho, rho, ALU.mult).then_inc(S["dve_chain"], 1)
            e.eng.wait_ge(S["dve_chain"], e.c["dve_chain"].next())
            cmul(e, q3, q4, cs, sn, cs, sn, q1, q2)
            cmul(e, wre, wim, q3, q4, q3, q4, q1, q2)
            for dst in (bT_re, bT_im, toep):
                for n in range(0, NP_, 4):
                    e.eng.wait_ge(S["tile_done"], e.c["tile"].next())
                    nc.vector.tensor_copy(dst[:, n:n + 4, :], by_block(e.result())).then_inc(S["tile_free"], 1)
                    e.eng.wait_ge(S["tile_free"], e.c["tile"].at())
            e.tick()

        def ssm_run_pe(e):
            for src in (bT_re, bT_im):
                for n in range(0, NP_, 4):
                    e.eng.wait_ge(S["tile_free"], e.c["tile"].at(-1))
                    o = e.bank()
                    for j in range(4):
                        ins = e.mm(blk(o, j), src[:, n + j, :], ushift[:, n + j, :])
                    ins.then_inc(S["tile_done"], 1)
            e.eng.wait_ge(S["states"], e.c["states"].next())
            for n in range(0, NP_, 4):
                e.eng.wait_ge(S["tile_free"], e.c["tile"].at(-1))
                o = e.bank()
                for j in range(4):
                    oo = blk(o, j)
                    e.mm(oo, toep[:, n + j, :], ushift[:, n + j, :], True, False)
                    e.mm(oo[:, 1:P], c_re[:, n + j, 4:8, :].rearrange("p l c -> p (l c)"), v_re[:, n + j, 0:P - 1],
                         False, False)
                    ins = e.mm(oo[:, 1:P], c_im[:, n + j, 4:8, :].rearrange("p l c -> p (l c)"),
                               v_im[:, n + j, 0:P - 1], False, True)
                ins.then_inc(S["tile_done"], 1)
            e.eng.wait_ge(S["gelu"], e.c["gelu"].next())
            for m in range(0, DC, 2):
                e.eng.wait_ge(S[e.landing()], e.landed())
                w = e.slot(ring)
                for j in range(4):
                    e.eng.wait_ge(S["tile_free"], e.c["tile"].at(-1))
                    e.dense(e.bank(), blocks(w, 4 * j, 4), [uT[:, k, :] for k in range(4)])

        def ssm_run_act(e):
            e.skip(12)
            for j in range(4):
                e.eng.wait_ge(S["skip_added"], e.c["skip_added"].next())
                nc.scalar.activation(uT[:, j, :], uT[:, j, :], ACT.Gelu_apprx_tanh)\
                    .then_inc(S["gelu_part"], 1)
            for m in range(DC):
                e.eng.wait_ge(S["tile_free"], e.c["tile"].next())
                e.eng.wait_ge(S["tile_done"], e.c["tile"].next())
                t = e.result()
                e.eng.wait_ge(S["tile_free"], e.c["tile"].at(-1))
                nc.scalar.activation(glu_g[:, m % 2, :], t, ACT.Sigmoid, bias=V("glu_b")[:, 8 + m:9 + m])\
                    .then_inc(S["tile_free"], 1)
                e.eng.wait_ge(S["tile_free"], e.c["tile"].at())

        y_sh = ssm_in_flat = None
        glu_a = toep.rearrange("p a b -> p (a b)").rearrange("p (a b) -> p a b", b=T)
        glu_g = bT_re.rearrange("p a b -> p (a b)").rearrange("p (a b) -> p a b", b=T)

        def ssm_run_dve(e):
            nc.vector.memset(turn_re[:, :, 0:1], 1.0).then_inc(S["dve_chain"], 1)
            e.eng.wait_ge(S["dve_chain"], e.c["dve_chain"].next())
            nc.vector.memset(turn_im[:, :, 0:1], 0.0).then_inc(S["dve_chain"], 1)
            e.eng.wait_ge(S["dve_chain"], e.c["dve_chain"].next())
            t1_ = decay4
            t2_ = xtmp
            n = 1
            while n < P:
                cmul(e, turn_re[:, :, n:2 * n], turn_im[:, :, n:2 * n], turn_re[:, :, 0:n], turn_im[:, :, 0:n],
                     bc(wre, n), bc(wim, n), t1_[:, :, 0:n], t2_[:, :, 0:n])
                cmul(e, q3, q4, wre, wim, wre, wim, q1, q2)
                nc.vector.tensor_copy(wre, q3).then_inc(S["dve_chain"], 1)
                e.eng.wait_ge(S["dve_chain"], e.c["dve_chain"].next())
                nc.vector.tensor_copy(wim, q4).then_inc(S["dve_chain"], 1)
                e.eng.wait_ge(S["dve_chain"], e.c["dve_chain"].next())
                n *= 2
            for dst in (v_re, v_im):
                for n in range(0, NP_, 4):
                    e.eng.wait_ge(S["tile_done"], e.c["tile"].next())
                    nc.vector.tensor_copy(dst[:, n:n + 4, :], by_block(e.result())).then_inc(S["tile_free"], 1)
                    e.eng.wait_ge(S["tile_free"], e.c["tile"].at())
            nc.vector.tensor_tensor(z_re, v_re, turn_re, ALU.mult).then_inc(S["dve_chain"], 1)
            e.eng.wait_ge(S["dve_chain"], e.c["dve_chain"].next())
            nc.vector.tensor_tensor(t2_, v_im, turn_im, ALU.mult).then_inc(S["dve_chain"], 1)
            e.eng.wait_ge(S["dve_chain"], e.c["dve_chain"].next())
            nc.vector.tensor_tensor(z_re, z_re, t2_, ALU.add).then_inc(S["dve_chain"], 1)
            e.eng.wait_ge(S["dve_chain"], e.c["dve_chain"].next())
            nc.vector.tensor_tensor(z_im, v_im, turn_re, ALU.mult).then_inc(S["dve_chain"], 1)
            e.eng.wait_ge(S["dve_chain"], e.c["dve_chain"].next())
            nc.vector.tensor_tensor(t2_, v_re, turn_im, ALU.mult).then_inc(S["dve_chain"], 1)
            e.eng.wait_ge(S["dve_chain"], e.c["dve_chain"].next())
            nc.vector.tensor_tensor(z_im, z_im, t2_, ALU.subtract).then_inc(S["dve_chain"], 1)
            e.eng.wait_ge(S["dve_chain"], e.c["dve_chain"].next())
            nc.vector.tensor_copy(decay4, bc(rho, P)).then_inc(S["dve_chain"], 1)
            e.eng.wait_ge(S["dve_chain"], e.c["dve_chain"].next())
            nc.vector.memset(decay4[:, :, 0:1], 0.0).then_inc(S["dve_chain"], 1)
            e.eng.wait_ge(S["dve_chain"], e.c["dve_chain"].next())

            def f2(ap):
                return ap.rearrange("p a b -> p (a b)")
            for z in (z_re, z_im):
                nc.vector.tensor_tensor_scan(f2(z), f2(decay4), f2(z), 0.0, ALU.mult, ALU.add).then_inc(S["dve_chain"], 1)
                e.eng.wait_ge(S["dve_chain"], e.c["dve_chain"].next())
            cmul(e, v_re, v_im, z_re, z_im, turn_re, turn_im, decay4, t2_)
            nc.vector.memset(e.ticks, 0.0).then_inc(S["states"], 1)
            for n in range(4):
                e.eng.wait_ge(S["tile_done"], e.c["tile"].next())
                nc.vector.tensor_copy(ysh[:, 4 * n:4 * n + 4, :], by_block(e.result())).then_inc(S["tile_free"], 1)
                e.eng.wait_ge(S["tile_free"], e.c["tile"].at())
            for q in range(4):
                for t in range(Q):
                    nc.vector.tensor_copy(
                 yT[32 * q:32 * q + 32, :, t::4],
                 ysh[32 * t:32 * t + 32, :, :].rearrange("p (j q) m -> p q j m", q=4)[:, q]).then_inc(S["dve_chain"], 1)
                    e.eng.wait_ge(S["dve_chain"], e.c["dve_chain"].next())
            for j in range(4):
                nc.vector.scalar_tensor_tensor(out=uT[:, j, :], in0=uT[:, j, :], scalar=V("s_d")[:, j:j + 1],
                                               in1=yT[:, j, :], op0=ALU.mult, op1=ALU.add).then_inc(S["skip_added"], 1)
            for j in range(4):
                e.eng.wait_ge(S["gelu_part"], e.c["gelu_part"].next())
            nc.vector.memset(e.ticks, 0.0).then_inc(S["gelu"], 1)
            for m in range(DC):
                ga_ = glu_a[:, m % 2, :]
                e.eng.wait_ge(S["tile_done"], e.c["tile"].next())
                nc.vector.tensor_scalar(ga_, e.result(), V("glu_b")[:, m:m + 1], None, ALU.add).then_inc(S["tile_free"], 1)
                e.eng.wait_ge(S["tile_free"], e.c["tile"].at())
                e.eng.wait_ge(S["tile_free"], e.c["tile"].next())
                nc.vector.tensor_tensor(ga_, ga_, glu_g[:, m % 2, :], ALU.mult).then_inc(S["dve_chain"], 1)
                e.eng.wait_ge(S["dve_chain"], e.c["dve_chain"].next())
                nc.vector.tensor_tensor(xT[:, m, :], xT[:, m, :], ga_, ALU.add).then_inc(S["dve_chain"], 1)
                e.eng.wait_ge(S["dve_chain"], e.c["dve_chain"].next())
            e.tick()

        xtmp = a(NP_, P)
        ysh, yT = quarters(0, hT), hT[:, 4:8, :]

        out_tok = Arena()(NB, D)

        def final_pe(e):
            for c in range(DC):
                e.eng.wait_ge(S["tile_free"], e.c["tile"].at(-1))
                o = e.bank()
                for b in range(NB):
                    ins = e.eng.transpose(blk(o, b), blk(hT[:, c, :], b), ident)
                ins.then_inc(S["tile_done"], 1)

        def final_dve(e):
            for c in range(DC):
                e.eng.wait_ge(S["tile_done"], e.c["tile"].next())
                nc.vector.tensor_copy(out_tok[:, :, P * c:P * c + P], by_block(e.result())).then_inc(S["tile_free"], 1)
                e.eng.wait_ge(S["tile_free"], e.c["tile"].at())
            e.tick()

        ticks = sb("ticks", [P, 64])
        engines = []

        def start(cls, name, eng):
            e = cls(name, eng, S, acc)
            e.tick_columns = ticks[:, :]
            engines.append(e)
            return e

        NORMS = dict(norm_mix=(xT, hT, DC, "norm_mix", D), norm_ffn=(xT, hT, DC, "norm_ffn", D),
                     norm_ple=(xT, hT, DC, "norm_ple", D), mix0=(xT, hT, DC, "mix0", D), ffn0=(xT, hT, DC, "ffn0", D),
                     mix1=(xT, hT, DC, "mix1", D), ffn1=(xT, hT, DC, "ffn1", D), final=(xT, hT, DC, "final", D),
                     mla_q=(cq, cq, 2, "mla_q", 256), mla_kv=(ckv, ckv, 1, "mla_kv", 128))

        STAGES = ["load", "norm_mix", "values", "attn", "decay", "delta", "merge", "residual", "norm_ffn", "router",
                  "experts", "norm_ple", "ple", "mix0", "glu", "mla_q", "mla_kv", "latent", "mla", "residual2", "ffn0",
                  "ffn_a", "mix1", "ssm_setup", "ssm_run", "ffn1", "ffn_b", "final", "out"]

        block = ctx.enter_context(nc.Block())

        @block.sync
        def _(sp):
            for n in range(RING):
                sp.dma_start(ring[:, n, :], stream[n]).then_inc(S["loaded%d" % n], 16)
            with sp.Fori(0, NF // RING - 1) as i:
                for j in range(RING):
                    sp.wait_ge(S["slot_free"], i * RING + (j + 2))
                    sp.dma_start(ring[:, j, :], stream[bass.ds(i * RING + (RING + j), 1)].rearrange("o p n -> p (o n)"))\
                        .then_inc(S["loaded%d" % j], 16)
            sp.wait_ge(S["stage"], len(STAGES))
            sp.dma_start(out.rearrange("o (b p) d -> p (o b) d", p=P), out_tok).then_inc(S["out"], 16)
            sp.wait_ge(S["out"], 16)

        @block.tensor
        def _(pe):
            e = start(Tensor, "pe", pe)

            def norm(name):
                e.eng.wait_ge(S["stage"], e.c["stage"].next())
                e.mark(name)
                norm_pe(e, NORMS[name][2])

            load_pe(e)
            norm("norm_mix")
            e.eng.wait_ge(S["stage"], e.c["stage"].next())
            e.mark("values")
            values_pe(e)
            e.eng.wait_ge(S["stage"], e.c["stage"].next())
            e.mark("attn")
            attn_pe(e)
            e.eng.wait_ge(S["stage"], e.c["stage"].next())
            e.mark("decay")
            decay_pe(e)
            e.eng.wait_ge(S["stage"], e.c["stage"].next())
            e.mark("delta")
            with loop(e, 4, fill=4, tile=56, squares=6, kq_ready=2, level=12, inverse=2, state=16, vnew=16):
                delta_pe(e)
            e.eng.wait_ge(S["stage"], e.c["stage"].next())
            e.mark("merge")
            merge_pe(e)
            e.eng.wait_ge(S["stage"], e.c["stage"].next())
            e.mark("residual")
            residual_pe(e, mergedT)
            norm("norm_ffn")
            e.eng.wait_ge(S["stage"], e.c["stage"].next())
            e.mark("router")
            router_pe(e)
            e.eng.wait_ge(S["stage"], e.c["stage"].next())
            e.mark("experts")
            experts_pe(e)
            norm("norm_ple")
            e.eng.wait_ge(S["stage"], e.c["stage"].next())
            e.mark("ple")
            ple_pe(e)
            norm("mix0")
            e.eng.wait_ge(S["stage"], e.c["stage"].next())
            e.mark("glu")
            glu_pe(e)
            norm("mla_q")
            norm("mla_kv")
            e.eng.wait_ge(S["stage"], e.c["stage"].next())
            e.mark("latent")
            latent_pe(e)
            e.eng.wait_ge(S["stage"], e.c["stage"].next())
            e.mark("mla")
            mla_pe(e)
            e.eng.wait_ge(S["stage"], e.c["stage"].next())
            e.mark("residual2")
            residual_pe(e, mixT)
            norm("ffn0")
            e.eng.wait_ge(S["stage"], e.c["stage"].next())
            e.mark("ffn_a")
            ffn_pe(e)
            norm("mix1")
            e.eng.wait_ge(S["stage"], e.c["stage"].next())
            e.mark("ssm_setup")
            ssm_setup_pe(e)
            e.eng.wait_ge(S["stage"], e.c["stage"].next())
            e.mark("ssm_run")
            ssm_run_pe(e)
            norm("ffn1")
            e.eng.wait_ge(S["stage"], e.c["stage"].next())
            e.mark("ffn_b")
            ffn_pe(e)
            norm("final")
            e.eng.wait_ge(S["stage"], e.c["stage"].next())
            e.mark("out")
            final_pe(e)

        @block.scalar
        def _(act):
            e = start(Engine, "act", act)

            def norm(name):
                e.eng.wait_ge(S["stage"], e.c["stage"].next())
                e.mark(name)
                norm_act(e, NORMS[name][0], NORMS[name][2])

            load_act(e)
            e.skip(8)
            norm("norm_mix")
            e.eng.wait_ge(S["stage"], e.c["stage"].next())
            e.mark("values")
            e.eng.wait_ge(S["stage"], e.c["stage"].next())
            e.mark("attn")
            attn_act(e)
            e.eng.wait_ge(S["stage"], e.c["stage"].next())
            e.mark("decay")
            decay_act(e)
            e.eng.wait_ge(S["stage"], e.c["stage"].next())
            e.mark("delta")
            with loop(e, 4, tile=56, filtered=6, pad_free=2, act_chain=6, decay_arg=2, delta_raw=2) as i:
                delta_act(e, lambda s: i * 2 + s)
            e.eng.wait_ge(S["stage"], e.c["stage"].next())
            e.mark("merge")
            merge_act(e)
            e.eng.wait_ge(S["stage"], e.c["stage"].next())
            e.mark("residual")
            e.skip(8)
            norm("norm_ffn")
            e.eng.wait_ge(S["stage"], e.c["stage"].next())
            e.mark("router")
            router_act(e)
            e.eng.wait_ge(S["stage"], e.c["stage"].next())
            e.mark("experts")
            experts_act(e)
            norm("norm_ple")
            e.eng.wait_ge(S["stage"], e.c["stage"].next())
            e.mark("ple")
            ple_act(e)
            norm("mix0")
            e.eng.wait_ge(S["stage"], e.c["stage"].next())
            e.mark("glu")
            glu_act(e)
            norm("mla_q")
            norm("mla_kv")
            e.eng.wait_ge(S["stage"], e.c["stage"].next())
            e.mark("latent")
            e.skip(8 + 9 + 8 + 4)
            e.eng.wait_ge(S["stage"], e.c["stage"].next())
            e.mark("mla")
            mla_act(e)
            e.eng.wait_ge(S["stage"], e.c["stage"].next())
            e.mark("residual2")
            e.skip(8)
            norm("ffn0")
            e.eng.wait_ge(S["stage"], e.c["stage"].next())
            e.mark("ffn_a")
            ffn_act(e)
            norm("mix1")
            e.eng.wait_ge(S["stage"], e.c["stage"].next())
            e.mark("ssm_setup")
            ssm_setup_act(e)
            e.eng.wait_ge(S["stage"], e.c["stage"].next())
            e.mark("ssm_run")
            ssm_run_act(e)
            norm("ffn1")
            e.eng.wait_ge(S["stage"], e.c["stage"].next())
            e.mark("ffn_b")
            ffn_act(e)
            norm("final")
            e.eng.wait_ge(S["stage"], e.c["stage"].next())
            e.mark("out")
            e.skip(8)

        @block.vector
        def _(dve):
            e = start(Vector, "dve", dve)

            def norm(name):
                src, dst, n, gain, width = NORMS[name]
                e.eng.wait_ge(S["stage"], e.c["stage"].next())
                e.mark(name)
                norm_dve(e, src, dst, n, V(gain), width, EPS)
                e.tick()

            load_dve(e)
            norm("norm_mix")
            e.eng.wait_ge(S["stage"], e.c["stage"].next())
            e.mark("values")
            values_dve(e)
            e.tick()
            e.eng.wait_ge(S["stage"], e.c["stage"].next())
            e.mark("attn")
            attn_dve(e)
            e.eng.wait_ge(S["stage"], e.c["stage"].next())
            e.mark("decay")
            decay_dve(e)
            e.eng.wait_ge(S["stage"], e.c["stage"].next())
            e.mark("delta")
            for h in H:
                nc.vector.memset(h.pad[:, :, 0:3], 0.0).then_inc(S["dve_chain"], 1)
                e.eng.wait_ge(S["dve_chain"], e.c["dve_chain"].next())
                nc.vector.memset(h.vnew, 0.0).then_inc(S["dve_chain"], 1)
                e.eng.wait_ge(S["dve_chain"], e.c["dve_chain"].next())
            with loop(e, 4, tile=56, root=4, exp_rows=2, decay=2, w_state=16, k_vnew=16, delta_out=2, level=12,
                      state=16, delta_raw=2, dve_chain=56) as i:
                delta_dve(e, lambda s: i * 2 + s)
            e.tick()
            e.eng.wait_ge(S["stage"], e.c["stage"].next())
            e.mark("merge")
            merge_dve(e)
            e.eng.wait_ge(S["stage"], e.c["stage"].next())
            e.mark("residual")
            residual_dve(e)
            e.tick()
            norm("norm_ffn")
            e.eng.wait_ge(S["stage"], e.c["stage"].next())
            e.mark("router")
            router_dve(e)
            e.eng.wait_ge(S["stage"], e.c["stage"].next())
            e.mark("experts")
            experts_dve(e)
            norm("norm_ple")
            e.eng.wait_ge(S["stage"], e.c["stage"].next())
            e.mark("ple")
            ple_dve(e)
            norm("mix0")
            e.eng.wait_ge(S["stage"], e.c["stage"].next())
            e.mark("glu")
            glu_dve(e)
            norm("mla_q")
            norm("mla_kv")
            e.eng.wait_ge(S["stage"], e.c["stage"].next())
            e.mark("latent")
            latent_dve(e)
            e.eng.wait_ge(S["stage"], e.c["stage"].next())
            e.mark("mla")
            mla_dve(e)
            e.eng.wait_ge(S["stage"], e.c["stage"].next())
            e.mark("residual2")
            residual_dve(e)
            e.tick()
            norm("ffn0")
            e.eng.wait_ge(S["stage"], e.c["stage"].next())
            e.mark("ffn_a")
            ffn_dve(e, "f0_w", "f0_b")
            norm("mix1")
            e.eng.wait_ge(S["stage"], e.c["stage"].next())
            e.mark("ssm_setup")
            ssm_setup_dve(e)
            e.eng.wait_ge(S["stage"], e.c["stage"].next())
            e.mark("ssm_run")
            ssm_run_dve(e)
            norm("ffn1")
            e.eng.wait_ge(S["stage"], e.c["stage"].next())
            e.mark("ffn_b")
            ffn_dve(e, "f1_w", "f1_b")
            norm("final")
            e.eng.wait_ge(S["stage"], e.c["stage"].next())
            e.mark("out")
            final_dve(e)

        for (a_, b_, c_) in zip(*(e.marks for e in engines)):
            assert a_ == b_ == c_, (a_, b_, c_)


def kernel(**inputs):
    import concourse.bacc as _bacc
    from concourse.bass_utils import run_bass_kernel_spmd as _run

    w = {k: np.asarray(v) for k, v in inputs.items()}
    arrays = {"x": np.ascontiguousarray(w["x"]), "p": np.ascontiguousarray(w["p"]), "stream": weight_stream(w),
              "vecs": vectors(w), "consts": constants(), "ssm": ssm_matrices(w)}
    nc = _bacc.Bacc("TRN2", target_bir_lowering=False, num_devices=1)
    args = {k: nc.dram_tensor(k + "_dram", a.shape, F32, kind="ExternalInput").ap() for k, a in arrays.items()}
    o = nc.dram_tensor("out_dram", (1, T, D), F32, kind="ExternalOutput").ap()
    program(nc, out=o, **args)
    r = _run(nc, [{k + "_dram": a for k, a in arrays.items()}], core_ids=[0])
    return r.results[0]["out_dram"]
```
